# Optimizing a Trainium2 kernel written in Bass

```python
import jax, jax.numpy as jnp
from jax import lax
import numpy as np

D_MODEL = 1024
BATCH = 1
SEQ = 256
DEPTH = 4

N_MIXERS = 3
N_FOX_LAYERS = (DEPTH + 2) // 3
N_HGRN_LAYERS = (DEPTH + 1) // 3
N_CONV_LAYERS = DEPTH // 3

FOX_HEADS = 16
FOX_HEAD_DIM = D_MODEL // FOX_HEADS
FOX_BLOCK = 128
FOX_IN_WIDTH = 3 * D_MODEL + FOX_HEADS
FORGET_BIAS_INIT = 1.0

HGRN_EXPAND = 128
HGRN_HEADS = D_MODEL // HGRN_EXPAND
HGRN_KEY_DIM = HGRN_EXPAND
HGRN_VAL_DIM = D_MODEL // HGRN_HEADS
HGRN_KEY_WIDTH = HGRN_HEADS * HGRN_KEY_DIM
HGRN_VAL_WIDTH = HGRN_HEADS * HGRN_VAL_DIM
HGRN_IN_WIDTH = 2 * HGRN_KEY_WIDTH + 2 * HGRN_VAL_WIDTH
HGRN_CHUNK = 64

CONV_WIDTH = 3

N_GROUPS = 4
EXPERTS_PER_GROUP = 8
N_EXPERTS = N_GROUPS * EXPERTS_PER_GROUP
TOP_K = 2
EXPERT_DIM = 256

DEEPNORM_ALPHA = (2 * DEPTH) ** 0.25
DEEPNORM_BETA = (8 * DEPTH) ** -0.25
LN_EPS = 1e-5
RMS_EPS = 1e-6

kernel_name = 'hybrid_fox_hgrn2_shortconv_hmoe_deepnorm'

def layer_norm(x, g, b):
    xf = x.astype(jnp.float32)
    mu = jnp.mean(xf, axis=-1, keepdims=True)
    var = jnp.mean(jnp.square(xf - mu), axis=-1, keepdims=True)
    return ((xf - mu) * lax.rsqrt(var + LN_EPS) * g + b).astype(x.dtype)

def forgetting_attention(x, w_in, b_f, w_out):
    bsz, t_len, _ = x.shape
    proj = x @ w_in
    q, k, v, f_logit = jnp.split(proj, [D_MODEL, 2 * D_MODEL, 3 * D_MODEL], axis=-1)

    def heads(t):
        return t.reshape(bsz, t_len, FOX_HEADS, FOX_HEAD_DIM).transpose(0, 2, 1, 3).astype(jnp.float32)

    q = heads(q) * (FOX_HEAD_DIM ** -0.5)
    k = heads(k)
    v = heads(v)
    log_f = jax.nn.log_sigmoid((f_logit + b_f).astype(jnp.float32))
    c = jnp.cumsum(log_f, axis=1).transpose(0, 2, 1)

    n_blocks = t_len // FOX_BLOCK
    q_blocks = q.reshape(bsz, FOX_HEADS, n_blocks, FOX_BLOCK, FOX_HEAD_DIM).transpose(2, 0, 1, 3, 4)
    c_blocks = c.reshape(bsz, FOX_HEADS, n_blocks, FOX_BLOCK).transpose(2, 0, 1, 3)
    qpos_blocks = jnp.arange(t_len).reshape(n_blocks, FOX_BLOCK)
    kpos = jnp.arange(t_len)

    def query_block(args):
        qb, cb, qp = args
        s = jnp.einsum('bhqd,bhkd->bhqk', qb, k) + (cb[..., :, None] - c[:, :, None, :])
        s = jnp.where(kpos[None, :] <= qp[:, None], s, -jnp.inf)
        p = jax.nn.softmax(s, axis=-1)
        return jnp.einsum('bhqk,bhkd->bhqd', p, v)

    o = lax.map(query_block, (q_blocks, c_blocks, qpos_blocks))
    o = o.transpose(1, 0, 3, 2, 4).reshape(bsz, t_len, D_MODEL).astype(x.dtype)
    return o @ w_out

def hgrn2(x, w_in, lower_bound, norm_g, w_out):
    bsz, t_len, _ = x.shape
    q, f_logit, i, g = jnp.split(
        x @ w_in,
        [HGRN_KEY_WIDTH, 2 * HGRN_KEY_WIDTH, 2 * HGRN_KEY_WIDTH + HGRN_VAL_WIDTH], axis=-1)
    f = lower_bound + (1.0 - lower_bound) * jax.nn.sigmoid(f_logit.astype(jnp.float32))
    log_f = jnp.log(f)
    k = 1.0 - f

    n_chunks = t_len // HGRN_CHUNK

    def chunks(t, d):
        return t.astype(jnp.float32).reshape(bsz, n_chunks, HGRN_CHUNK, HGRN_HEADS, d).transpose(1, 0, 3, 2, 4)

    qc = chunks(q, HGRN_KEY_DIM)
    kc = chunks(k, HGRN_KEY_DIM)
    gc = chunks(log_f, HGRN_KEY_DIM)
    ic = chunks(i, HGRN_VAL_DIM)
    causal = jnp.tril(jnp.ones((HGRN_CHUNK, HGRN_CHUNK), dtype=bool))

    def step(state, inp):
        qb, kb, gb, ib = inp
        b = jnp.cumsum(gb, axis=-2)
        diff = b[:, :, :, None, :] - b[:, :, None, :, :]
        decay = jnp.exp(jnp.where(causal[:, :, None], diff, -jnp.inf))
        scores = jnp.einsum('bhtk,bhsk,bhtsk->bhts', qb, kb, decay)
        o = (jnp.einsum('bhts,bhsv->bhtv', scores, ib)
             + jnp.einsum('bhtk,bhkv->bhtv', qb * jnp.exp(b), state))
        b_last = b[:, :, -1:, :]
        state = (jnp.exp(b_last[:, :, 0, :])[..., None] * state
                 + jnp.einsum('bhsk,bhsv->bhkv', kb * jnp.exp(b_last - b), ib))
        return state, o

    s0 = jnp.zeros((bsz, HGRN_HEADS, HGRN_KEY_DIM, HGRN_VAL_DIM), jnp.float32)
    _, o = lax.scan(step, s0, (qc, kc, gc, ic))
    o = o.transpose(1, 0, 3, 2, 4).reshape(bsz, t_len, HGRN_HEADS, HGRN_VAL_DIM)
    o = o * lax.rsqrt(jnp.mean(jnp.square(o), axis=-1, keepdims=True) + RMS_EPS) * norm_g
    o = (o.reshape(bsz, t_len, HGRN_VAL_WIDTH) * jax.nn.silu(g.astype(jnp.float32))).astype(x.dtype)
    return o @ w_out

def short_conv(x, w_in, conv_w, w_out):
    b_gate, c_gate, h = jnp.split(x @ w_in, 3, axis=-1)
    z = c_gate * h
    y = lax.conv_general_dilated(
        z, conv_w[:, None, :], window_strides=(1,), padding=((CONV_WIDTH - 1, 0),),
        dimension_numbers=('NWC', 'WIO', 'NWC'), feature_group_count=D_MODEL)
    return (b_gate * y) @ w_out

def hierarchical_moe(x, w_group, b_group, w_expert, b_expert, w_gate, w_up, w_down):
    bsz, t_len, _ = x.shape
    grp_logits = (x @ w_group).astype(jnp.float32) + b_group
    grp_prob = jax.nn.softmax(grp_logits, axis=-1)
    g_sel = jnp.argmax(grp_logits, axis=-1)
    grp_w = jnp.max(grp_prob, axis=-1, keepdims=True)
    exp_logits = ((x @ w_expert).astype(jnp.float32) + b_expert).reshape(
        bsz, t_len, N_GROUPS, EXPERTS_PER_GROUP)
    in_grp = jnp.einsum('btg,btge->bte', jax.nn.one_hot(g_sel, N_GROUPS, dtype=jnp.float32), exp_logits)
    p_in = jax.nn.softmax(in_grp, axis=-1)
    top_p, top_i = lax.top_k(p_in, TOP_K)
    weights = top_p / jnp.sum(top_p, axis=-1, keepdims=True) * grp_w
    expert_ids = g_sel[..., None] * EXPERTS_PER_GROUP + top_i
    gates = jnp.sum(jax.nn.one_hot(expert_ids, N_EXPERTS, dtype=jnp.float32) * weights[..., None], axis=-2)
    hg = jnp.einsum('btd,edf->btef', x, w_gate)
    hu = jnp.einsum('btd,edf->btef', x, w_up)
    h = jax.nn.silu(hg) * hu * gates[..., None].astype(x.dtype)
    return jnp.einsum('btef,efd->btd', h, w_down)

def _normal(key, shape, scale):
    return jax.random.normal(key, shape, jnp.float32) * scale

def setup_inputs(seed: int = 0) -> dict:
    key = jax.random.key(seed)
    ks = jax.random.split(key, 22)
    d = D_MODEL
    return {
        'x': _normal(ks[0], (BATCH, SEQ, d), 1.0),
        'ln_mix_g': 1.0 + _normal(ks[1], (DEPTH, d), 0.02),
        'ln_mix_b': _normal(ks[2], (DEPTH, d), 0.02),
        'ln_ffn_g': 1.0 + _normal(ks[3], (DEPTH, d), 0.02),
        'ln_ffn_b': _normal(ks[4], (DEPTH, d), 0.02),
        'fox_w_in': _normal(ks[5], (N_FOX_LAYERS, d, FOX_IN_WIDTH), d ** -0.5),
        'fox_b_f': FORGET_BIAS_INIT + _normal(ks[6], (N_FOX_LAYERS, FOX_HEADS), 0.1),
        'fox_w_out': _normal(ks[7], (N_FOX_LAYERS, d, d), d ** -0.5 * DEEPNORM_BETA),
        'hgrn_w_in': _normal(ks[8], (N_HGRN_LAYERS, d, HGRN_IN_WIDTH), d ** -0.5),
        'hgrn_lb_logits': _normal(ks[9], (DEPTH, HGRN_KEY_WIDTH), 0.1),
        'hgrn_norm_g': 1.0 + _normal(ks[10], (N_HGRN_LAYERS, HGRN_VAL_DIM), 0.02),
        'hgrn_w_out': _normal(ks[11], (N_HGRN_LAYERS, HGRN_VAL_WIDTH, d), HGRN_VAL_WIDTH ** -0.5 * DEEPNORM_BETA),
        'conv_w_in': _normal(ks[12], (N_CONV_LAYERS, d, 3 * d), d ** -0.5),
        'conv_w': _normal(ks[13], (N_CONV_LAYERS, CONV_WIDTH, d), CONV_WIDTH ** -0.5),
        'conv_w_out': _normal(ks[14], (N_CONV_LAYERS, d, d), d ** -0.5 * DEEPNORM_BETA),
        'moe_w_group': _normal(ks[15], (DEPTH, d, N_GROUPS), d ** -0.5),
        'moe_b_group': _normal(ks[16], (DEPTH, N_GROUPS), 0.01),
        'moe_w_expert': _normal(ks[17], (DEPTH, d, N_EXPERTS), d ** -0.5),
        'moe_b_expert': _normal(ks[18], (DEPTH, N_EXPERTS), 0.01),
        'moe_w_gate': _normal(ks[19], (DEPTH, N_EXPERTS, d, EXPERT_DIM), d ** -0.5),
        'moe_w_up': _normal(ks[20], (DEPTH, N_EXPERTS, d, EXPERT_DIM), d ** -0.5),
        'moe_w_down': _normal(ks[21], (DEPTH, N_EXPERTS, EXPERT_DIM, d), EXPERT_DIM ** -0.5 * DEEPNORM_BETA),
    }

def reference(x, ln_mix_g, ln_mix_b, ln_ffn_g, ln_ffn_b,
              fox_w_in, fox_b_f, fox_w_out,
              hgrn_w_in, hgrn_lb_logits, hgrn_norm_g, hgrn_w_out,
              conv_w_in, conv_w, conv_w_out,
              moe_w_group, moe_b_group, moe_w_expert, moe_b_expert,
              moe_w_gate, moe_w_up, moe_w_down):
    lb_prob = jax.nn.softmax(hgrn_lb_logits.astype(jnp.float32), axis=0)
    lower_bounds = jnp.cumsum(lb_prob, axis=0) - lb_prob[0]

    for layer in range(DEPTH):
        kind = layer % N_MIXERS
        j = layer // N_MIXERS
        if kind == 0:
            mixed = forgetting_attention(x, fox_w_in[j], fox_b_f[j], fox_w_out[j])
        elif kind == 1:
            mixed = hgrn2(x, hgrn_w_in[j], lower_bounds[layer], hgrn_norm_g[j], hgrn_w_out[j])
        else:
            mixed = short_conv(x, conv_w_in[j], conv_w[j], conv_w_out[j])
        x = layer_norm(DEEPNORM_ALPHA * x + mixed, ln_mix_g[layer], ln_mix_b[layer])
        ffn = hierarchical_moe(x, moe_w_group[layer], moe_b_group[layer], moe_w_expert[layer],
                               moe_b_expert[layer], moe_w_gate[layer], moe_w_up[layer], moe_w_down[layer])
        x = layer_norm(DEEPNORM_ALPHA * x + ffn, ln_ffn_g[layer], ln_ffn_b[layer])
    return x


_drawn_inputs = setup_inputs


def setup_inputs(seed=0):
    import zlib

    import numpy as np

    out = dict(_drawn_inputs(seed))
    spreads = {}
    factors = {'fox_b_f': 3.877,
     'hgrn_lb_logits': 6.402,
     'hgrn_norm_g': 7.12,
     'moe_b_group': 8.0,
     'moe_b_expert': 8.0}
    for name, (base, spread) in spreads.items():
        noise = np.random.default_rng([zlib.crc32(name.encode()), seed]).standard_normal(out[name].shape)
        drawn = base * np.exp(spread * noise) if base else spread * noise
        out[name] = __import__('jax').numpy.asarray(drawn.astype(out[name].dtype))
    for name, factor in factors.items():
        out[name] = (out[name] * factor).astype(out[name].dtype)
    return out
```

```python
import math
from contextlib import ExitStack

import numpy as np

import concourse.bass as bass
from concourse import mybir

F32 = mybir.dt.float32
I32 = mybir.dt.int32
ACT = mybir.ActivationFunctionType
ALU = mybir.AluOpType
AX = mybir.AxisListType.X

P = 128
D = 1024
KD = D // P
T = 256
TC = T // P
DEPTH = 4
HEADS, HD = 16, 64
HH, HK = 8, 128
CW = 3
NG, EG = 4, 8
NE = NG * EG
ED = 256
FC = ED // P
HB = 512
NH = D // HB
LN_EPS, RMS_EPS = 1e-5, 1e-6
ALPHA = float((2 * DEPTH) ** 0.25)
BIG = 1e30

QE = 4
W = P // QE
NQ = NE // QE
NW = T // W
GU = 4
QU = GU + FC

UNIT = 4096
RING = 6
assert QU % RING == 0
WINDOW_LIMIT = W
MORE = (NW - 1) * NQ
FREE = 1
KINDS = [layer % 3 for layer in range(DEPTH)]
IN_UNITS = {0: 6, 1: 8, 2: 6}
HGRN_ORDER = [2, 3, 0, 1, 4, 5, 6, 7]
MIX_UNITS = {k: n + NH for k, n in IN_UNITS.items()}
MIX_BASE = [sum(MIX_UNITS[k] for k in KINDS[:l]) + NQ * QU * l for l in range(DEPTH)]
MOE_BASE = [MIX_BASE[l] + MIX_UNITS[KINDS[l]] for l in range(DEPTH)]

LEVELS = [64, 32, 16, 8, 4, 2, 1]
NL = len(LEVELS) + 1


def constants():
    i, j = np.arange(P)[:, None], np.arange(P)[None, :]
    parts = {
        "tri": i <= j, "ones": np.ones((P, P)), "strict": i < j,
        "alpha": np.eye(P) * ALPHA,
        "causal": np.concatenate([(j > i) * BIG, np.zeros((P, P)), (j > i) * BIG], 1),
        "iota": np.broadcast_to(np.arange(W), (P, W)),
        "rev": np.broadcast_to(EG - np.arange(EG), (P, EG)),
    }
    spans, masks = [], []
    for m in LEVELS:
        block_i, block_j = i // (2 * m), j // (2 * m)
        mid = block_j * 2 * m + m
        later = (j >= mid) & (i >= mid) & (i <= j)
        earlier = (j < mid) & (i > j) & (i < mid)
        spans.append(later | earlier)
        masks.append((block_i == block_j) & (i < mid) & (j >= mid))
    parts["spans"] = np.concatenate(spans + [i > j], 1)
    parts["masks"] = np.concatenate(masks, 1)
    parts["ident"] = np.eye(P)
    at, n = {}, 0
    for name, a in parts.items():
        at[name] = (n, n + a.shape[1])
        n += a.shape[1]
    return np.concatenate([np.asarray(a, np.float32) for a in parts.values()], 1), at


CONST, CONST_AT = constants()


class Fills:

    def __init__(self):
        self.no, self.bank, self.drainer, self.count = {}, {}, {}, {}
        self.of = {"A": 0, "V": 0}
        self.user, self.before = {}, {}

    def add(self, key, bank, drainer):
        self.no[key] = len(self.no) + 1
        self.bank[key], self.drainer[key] = bank, drainer
        self.of[drainer] += 1
        self.count[key] = self.of[drainer]
        self.before[key] = self.user.get(bank)
        self.user[bank] = key

    def mark(self, name, banks):
        self.before[name] = [self.user[b] for b in banks if b in self.user]


def plan():
    f = Fills()
    turn = [0]

    def rot(n, base=0):
        turn[0] += 1
        return base + turn[0] % n

    def transposed_x(j):
        for c in range(TC):
            for half in range(2):
                f.add(("xT", j, c, half), rot(4), "V" if (c, half) == (1, 1) else "A")

    transposed_x(-1)
    for l in range(DEPTH):
        kind = KINDS[l]
        if kind == 0:
            f.add(("f", l), rot(8), "V")
            for name, drainer in (("q", "A"), ("k", "V")):
                for m in range(4):
                    f.add((name, l, m), rot(8), drainer)
            f.add(("cum", l), rot(8), "V")
            for h in range(NH):
                for c in range(TC):
                    f.add(("v", l, h, c), rot(8), "A")
            for h in range(HEADS + 2):
                if h < HEADS:
                    f.add(("S", l, h), rot(8), "V")
                if 1 <= h <= HEADS:
                    f.add(("PT", l, h - 1), rot(8), "A")
                if h >= 2:
                    f.add(("O", l, h - 2), rot(8), "V")
        elif kind == 1:
            for h in range(NH):
                f.add(("lb", l, h), rot(8), "A")
                f.add(("omlb", l, h), rot(8), "A")
            for h in range(NH):
                for c in range(TC):
                    f.add(("fg", l, h, c), rot(8), "A")
            for m in range(4):
                f.add(("q", l, m), rot(8), "A")
            for c in range(TC):
                for half in range(2):
                    f.add(("kT", l, c, half), rot(8), "A")
            for name in "ig":
                for h in range(NH):
                    for c in range(TC):
                        f.add((name, l, h, c), rot(8), "A")
            for h in range(HH + 2):
                if h < HH:
                    for c in range(TC):
                        for b in range(2):
                            f.add(("E", l, h, c, b), rot(8), "A")
                if 1 <= h <= HH:
                    f.add(("X", l, h - 1), rot(8), "A")
                    for c in range(TC):
                        for b in range(2):
                            f.add(("sc", l, h - 1, c, b), rot(8), "V")
                if h >= 2:
                    f.add(("pv", l, h - 2), rot(8), "V")
        else:
            for name, drainer in (("b", "A"), ("c", "A"), ("h", "V")):
                for m in range(4):
                    f.add((name, l, m), rot(8), drainer)
        if kind != 2:
            for c in range(TC):
                for half in range(2):
                    f.add(("oT", l, c, half), rot(4), "AV"[half])
        f.mark(("z banks", l), range(4, 8))
        transposed_x(2 * l)
        f.add(("logits", l), rot(4), "V")
        f.add(("rank", l), rot(4), "V")
        f.mark(("moe banks", l), range(4))
        if l < DEPTH - 1:
            transposed_x(2 * l + 1)
    return f


FILLS = plan()


def build(nc, a, out):
    with ExitStack() as ctx:
        def sb(name, shape, dt=F32):
            return ctx.enter_context(nc.sbuf_tensor(name, shape, dt))

        def sem(name):
            return ctx.enter_context(nc.semaphore(name))

        ring = sb("ring", [P, RING, UNIT])
        x = sb("x", [P, TC, D])
        xT = sb("xT", [P, KD, T])
        affine = sb("affine", [P, 2, D])
        const = sb("const", [P, CONST.shape[1]])
        work = sb("work", [P, 12288])
        extra = sb("extra", [P, 6144])
        small = sb("small", [P, 512])
        w_router = sb("w_router", [P, KD, NG + NE])
        b_router = sb("b_router", [P, DEPTH, NG + NE])
        taps = sb("taps", [P, CW, KD])
        most = sb("most", [P, DEPTH], I32)
        psum = ctx.enter_context(nc.psum_tensor("psum", [P, 8, HB], F32))

        def table(name):
            return const[:, CONST_AT[name][0]:CONST_AT[name][1]]

        ident, ones, tri, strict = (table(n) for n in ("ident", "ones", "tri", "strict"))
        alpha_i, causal, iota, rev = (table(n) for n in ("alpha", "causal", "iota", "rev"))
        spans = table("spans")
        masks = const[:, CONST_AT["masks"][0]:CONST_AT["ident"][1]]

        def region(t, at, shape):
            n = int(np.prod(shape))
            v = t[:, at:at + n]
            if len(shape) == 1:
                return v
            names = "abcd"[:len(shape)]
            spec = f"p ({' '.join(names)}) -> p {' '.join(names)}"
            return v.rearrange(spec, **{k: s for k, s in zip(names[:-1], shape[:-1])})

        qa = region(work, 0, [HEADS, T])
        ka = region(work, 4096, [HEADS, T])
        v_sb = region(work, 8192, [TC, D])
        o_sb = region(work, 10240, [TC, D])
        sm = region(extra, 0, [2, 384])
        pexp = region(extra, 768, [2, 384])
        pT = region(extra, 1536, [2, 384])
        cum = region(extra, 2304, [2, T])
        lf = region(extra, 2816, [TC, HEADS])
        lf_t = region(extra, 2848, [TC, HEADS])
        lf_z = region(extra, 2880, [TC, HEADS])
        wf = region(extra, 3072, [KD, HEADS])
        bf = region(extra, 3200, [HEADS])
        nmax = region(extra, 2944, [2, TC])
        psums = region(extra, 3216, [HEADS, TC])
        rsum = region(extra, 2952, [2, TC])
        qT = region(work, 0, [HH, T])
        kT = region(work, 2048, [HH, T])
        fg = region(work, 4096, [TC, D])
        i_sb = region(work, 6144, [TC, D])
        sg_sb = region(work, 8192, [TC, D])
        lbs = region(work, 10240, [2, D])
        lb_diag = region(work, 6144, [2, KD, P])
        qk = region(extra, 0, [2, TC, NL, P])
        masked = region(extra, 4096, [NL, P])
        scT = region(extra, 5120, [2, 3, P])
        square = region(extra, 5888, [TC, P])
        norm_g = region(small, 384, [HK])
        ssq = region(small, 336, [TC, HH])
        ssq_t = region(small, 352, [TC, HH])
        rms = region(small, 368, [TC, HH])
        bT = region(work, 0, [KD, T])
        cT = region(work, 2048, [KD, T])
        yT = region(work, 4096, [KD, T])
        PADT = T + CW - 1
        zT = region(work, 6144, [KD, PADT])
        xw = region(work, 0, [2, KD, P])
        sel = region(work, 2048, [2, TC, P])
        selg = region(work, 2560, [2, TC, P])
        silu_g = region(work, 3072, [ED])
        h_sb = region(work, 3328, [ED])
        hT = region(work, 3584, [FC + TC, P])
        y_sb = region(work, 4096, [D])
        stats = region(small, 0, [TC, 2, 6])
        mv = region(small, 24, [TC, 2])
        ve = region(small, 28, [TC])
        lnv = region(small, 30, [TC])
        rstd = region(small, 32, [TC])
        nt = region(small, 34, [TC])
        lg = region(small, 40, [TC, NG + NE])
        gm = region(small, 112, [TC])
        eq = region(small, 114, [TC, EG])
        vv = region(small, 130, [TC, EG])
        vm = region(small, 146, [TC])
        og = region(small, 148, [TC, NG])
        ig = region(small, 156, [TC, EG])
        o1 = region(small, 172, [TC, EG])
        o2 = region(small, 188, [TC, EG])
        m1 = region(small, 204, [TC])
        m2 = region(small, 206, [TC])
        dge = region(small, 208, [TC, NG + 1])
        ege = region(small, 218, [TC, NG + 1])
        gsum = region(small, 228, [TC])
        den = region(small, 230, [TC])
        w1 = region(small, 232, [TC])
        w2 = region(small, 234, [TC])
        cmax = region(small, 236, [1])
        lb_in_sb = region(small, 240, [DEPTH, KD])
        lb_e = region(small, 272, [DEPTH, KD])
        lb_m = region(small, 304, [KD])
        lb_s = region(small, 312, [KD])
        lb_v = region(small, 320, [2, KD])
        picked = region(extra, 0, [TC, NE])
        gates = region(extra, 64, [TC, NE])
        rank = region(extra, 128, [TC, NE])
        a1 = region(extra, 192, [TC, NE])
        a2 = region(extra, 256, [TC, NE])
        le = region(extra, 320, [TC, NE])

        const_in, x_in, b_in, w_r_in, wf_in, taps_in, lb_in, cum_in, norm_in = (
            sem(n) for n in ("const_in", "x_in", "b_in", "w_r_in", "wf_in", "taps_in", "lb_in", "cum_in", "norm_in"))
        affine_in = sem("affine_in")
        unit_in = [sem(f"unit_in{s}") for s in range(RING)]
        unit_used, out_half0 = sem("unit_used"), sem("out_half0")
        bank_filled = sem("bank_filled")
        drained_by = {"A": sem("drained_act"), "V": sem("drained_dve")}
        x_ready, z_ready = sem("x_ready"), sem("z_ready")
        var_ready, seed_ready = sem("var_ready"), sem("seed_ready")
        ones_set = sem("ones_set")
        dve_step, act_step = sem("dve_step"), sem("act_step")
        lfz_ready, lfe_ready, lf_ready = sem("lfz_ready"), sem("lfe_ready"), sem("lf_ready")
        nmax_ready, p_ready = sem("nmax_ready"), sem("p_ready")
        fg_ready, log_ready = sem("fg_ready"), sem("log_ready")
        lbx_ready, lbe_ready, diag_ready = sem("lbx_ready"), sem("lbe_ready"), sem("diag_ready")
        sg_ready, qd_ready, kd_ready, sc_ready, ssq_ready, on_ready = (
            sem(n) for n in ("sg_ready", "qd_ready", "kd_ready", "sc_ready", "ssq_ready", "on_ready"))
        ssqe_ready, rms_seed = sem("ssqe_ready"), sem("rms_seed")
        pad_set, y_conv = sem("pad_set"), sem("y_conv")
        dge_ready, ege_ready, picked_ready, most_ready = (sem(n) for n in ("dge_ready", "ege_ready", "picked_ready", "most_ready"))
        MOE = ("sel_ready", "gathered", "xw_ready", "silu_ready", "h_ready", "hT_filled", "hT_ready",
               "y_filled", "y0_ready", "y1_ready", "sel_made")
        first = {n: sem(f"{n}_1") for n in MOE}
        more = {n: sem(f"{n}_n") for n in MOE + ("combined", "shifted")}
        first["unit_used"], more["unit_used"] = unit_used, sem("unit_used_n")
        more_in = [sem(f"more_in{s}") for s in range(RING)]
        out_written = sem("out_written")

        def spare(sems):
            return FREE if sems is more else 0

        def filled(key):
            return bank_filled, FILLS.no[key]

        def drained(key):
            return drained_by[FILLS.drainer[key]], FILLS.count[key]

        def bank(key, n=HB, at=0):
            return psum[:, FILLS.bank[key], at:at + n]

        def landed(n):
            return unit_in[n % RING], 32 * (n // RING + 1)

        def slot(n):
            return ring[:, n % RING, :]

        def used(n):
            for l in range(DEPTH):
                if MOE_BASE[l] <= n < MOE_BASE[l] + NQ * QU:
                    return unit_used, NQ * QU * l + n - MOE_BASE[l] + 1
                if MIX_BASE[l] <= n < MOE_BASE[l]:
                    m, kind = n - MIX_BASE[l], KINDS[l]
                    if m >= IN_UNITS[kind]:
                        return (out_half0, l + 1) if m == IN_UNITS[kind] else (z_ready, TC * (2 * l + 1))
                    name = {0: "qqkkvv", 1: "ffqqiigg", 2: "bbcchh"}[kind][m]
                    if name in "vig" or (kind == 1 and name == "f"):
                        return filled((("fg" if name == "f" else name), l, m % 2, TC - 1))
                    return filled((name, l, 2 * (m % 2) + 1))

        def more_path(eng, l, runs, body):
            eng.wait_ge(most_ready, l + 1)
            over = eng.value_load(most[0:1, l:l + 1], min_val=0, max_val=1)
            with eng.If(over > 0):
                body(l, runs)
            return over + runs

        block = ctx.enter_context(nc.Block())

        @block.sync
        def _(sp):
            w_in = {0: a["fox_w_in"], 1: a["hgrn_w_in"], 2: a["conv_w_in"]}
            w_out = {0: a["fox_w_out"], 1: a["hgrn_w_out"], 2: a["conv_w_out"]}

            def mixer(l):
                kind, j = KINDS[l], KINDS[:l].count(KINDS[l])
                for m in range(MIX_UNITS[kind]):
                    n = MIX_BASE[l] + m
                    if m < IN_UNITS[kind]:
                        col = (HGRN_ORDER[m] if kind == 1 else m) * HB
                        src = w_in[kind][j].rearrange("(p k) c -> p k c", k=KD)[:, :, col:col + HB]
                    else:
                        col = (m - IN_UNITS[kind]) * HB
                        src = w_out[kind][j].rearrange("(k p) c -> p k c", p=P)[:, :, col:col + HB]
                    dst = slot(n).rearrange("p (k c) -> p k c", k=KD)
                    if n >= RING:
                        sp.wait_ge(*used(n - RING))
                    for g in range(2):
                        sp.dma_start(dst[:, 4 * g:4 * g + 4, :],
                                     src[:, 4 * g:4 * g + 4, :]).then_inc(unit_in[n % RING], 16)

            def quad_unit(l, e0, u, s, into):
                if u < GU:
                    dst = ring[:, s, :].rearrange("p (t e k) -> p t e k", t=2, e=QE)
                    step = KD // GU * ED
                    for t, w in enumerate((a["moe_w_gate"], a["moe_w_up"])):
                        src = w[l, bass.ds(e0, QE)].rearrange("e (p k) f -> p e (k f)", p=P)
                        sp.dma_start(dst[:, t], src[:, :, u * step:(u + 1) * step]).then_inc(into, 16)
                else:
                    dst = ring[:, s, :].rearrange("p (e c) -> p e c", e=QE)
                    for g in range(2):
                        src = a["moe_w_down"][l, bass.ds(e0 + 2 * g, 2)].rearrange("e (j p) c -> p j e c", p=P)
                        sp.dma_start(dst[:, 2 * g:2 * g + 2], src[:, u - GU]).then_inc(into, 16)

            def experts(l):
                for u in range(QU):
                    n = MOE_BASE[l] + u
                    sp.wait_ge(*used(n - RING))
                    quad_unit(l, 0, u, n % RING, unit_in[n % RING])
                with sp.Fori(1, NQ) as q:
                    for u in range(QU):
                        s = (MOE_BASE[l] + u) % RING
                        sp.wait_ge(unit_used, q * QU + (NQ * QU * l + u + 1 - RING))
                        quad_unit(l, q * QE, u, s, unit_in[s])

            def experts_more(l, runs):
                sp.wait_ge(unit_used, NQ * QU * (l + 1))
                with sp.Fori(0, NW - 1) as w:
                    with sp.Fori(0, NQ) as q:
                        sp.wait_ge(more["unit_used"], runs * (MORE * QU) + w * (NQ * QU) + q * QU + FREE)
                        for u in range(QU):
                            s = (MOE_BASE[l] + u) % RING
                            quad_unit(l, q * QE, u, s, more_in[s])

            runs = 0
            for l in range(DEPTH):
                mixer(l)
                experts(l)
                runs = more_path(sp, l, runs, experts_more)
                sp.wait_ge(more["unit_used"], runs * (MORE * QU) + FREE)
            for c in range(TC):
                sp.wait_ge(x_ready, TC * (2 * DEPTH - 1) + c + 1)
                sp.dma_start(out[0, c * P:(c + 1) * P, :], x[:, c, :]).then_inc(out_written, 16)
            sp.wait_ge(out_written, 16 * TC)

        @block.gpsimd
        def _(pool):
            pool.dma_start(lb_in_sb, a["hgrn_lb_logits"].rearrange("r (p k) -> p r k", k=KD)).then_inc(lb_in, 16)
            pool.dma_start(b_router[:, :, 0:NG], a["moe_b_group"].partition_broadcast(P)).then_inc(b_in, 16)
            pool.dma_start(b_router[:, :, NG:], a["moe_b_expert"].partition_broadcast(P)).then_inc(b_in, 16)
            pool.dma_start(norm_g, a["hgrn_norm_g"][0].partition_broadcast(P)).then_inc(norm_in, 16)
            for w in range(CW):
                pool.dma_start(taps[:, w, :], a["conv_w"][0, w].rearrange("(k p) -> p k", p=P),
                               allow_slow_non_contiguous=True).then_inc(taps_in, 16)

            def load_affine(j):
                l, names = j // 2, (("ln_mix_g", "ln_mix_b"), ("ln_ffn_g", "ln_ffn_b"))[j % 2]
                if j:
                    pool.wait_ge(x_ready, TC * j)
                for g, name in enumerate(names):
                    pool.dma_start(affine[:, g, :], a[name][l].partition_broadcast(P)).then_inc(affine_in, 16)

            for l in range(DEPTH):
                kind, j = KINDS[l], KINDS[:l].count(KINDS[l])
                if kind == 0:
                    if j:
                        pool.wait_ge(*filled(("f", l - 3)))
                        pool.wait_ge(drained_by["V"], FILLS.count[("f", l - 3)])
                    pool.dma_start(wf, a["fox_w_in"][j].rearrange("(p k) c -> p k c", k=KD)[:, :, 3 * D:]).then_inc(wf_in, 16)
                    pool.dma_start(bf, a["fox_b_f"][j].partition_broadcast(P)).then_inc(wf_in, 16)
                load_affine(2 * l)
                if l:
                    pool.wait_ge(*filled(("logits", l - 1)))
                pool.dma_start(w_router[:, :, 0:NG], a["moe_w_group"][l].rearrange("(p k) c -> p k c", k=KD)).then_inc(w_r_in, 16)
                pool.dma_start(w_router[:, :, NG:], a["moe_w_expert"][l].rearrange("(p k) c -> p k c", k=KD)).then_inc(w_r_in, 16)
                if kind == 0:
                    nc.gpsimd.memset(qa[64:66, :, :], 1.0).then_inc(ones_set, 1)
                    nc.gpsimd.memset(ka[64:66, :, :], 1.0).then_inc(ones_set, 1)
                    pool.wait_ge(ones_set, 2 * (j + 1))
                    pool.wait_ge(*drained(("cum", l)))
                    pool.dma_start(qa[65:66, :, :], cum[0:HEADS, 0:1, :]).then_inc(cum_in, 16)
                    pool.dma_start(ka[64:65, :, :], cum[0:HEADS, 1:2, :]).then_inc(cum_in, 16)
                elif kind == 1:
                    for h in range(HH):
                        pool.wait_ge(*drained(("E", l, h, TC - 1, 1)))
                        for i, m in enumerate(LEVELS):
                            e = qk[:, h % 2, :, i, :].rearrange("p c (b s m) -> p c b s m", s=2, m=m)[:, :, :, 0, :]
                            k = kT[:, h, :].rearrange("p (c b s m) -> p c b s m", c=TC, s=2, m=m)[:, :, :, 0, :]
                            nc.gpsimd.tensor_tensor(e, e, k, ALU.mult)
                        e = qk[:, h % 2, 0, NL - 1, :]
                        nc.gpsimd.tensor_tensor(e, e, kT[:, h, 0:P], ALU.mult).then_inc(kd_ready, 1)
                else:
                    nc.gpsimd.memset(zT[:, :, 0:CW - 1], 0.0).then_inc(pad_set, 1)
                load_affine(2 * l + 1)

        @block.tensor
        def _(pe):
            for s in (first["hT_filled"], more["hT_filled"], more["unit_used"], more["combined"]):
                pe.sem_inc(s, FREE)
            pe.wait_ge(const_in, 16)

            def free(key):
                before = FILLS.before[key]
                for b in before if isinstance(before, list) else [before] if before else []:
                    pe.wait_ge(*drained(b))

            def transposes(key, parts):
                free(key)
                for i, t in enumerate(parts):
                    last = nc.tensor.transpose(bank(key, P, i * P), t, ident)
                last.then_inc(bank_filled, 1)

            def x_transposes(j):
                for c in range(TC):
                    if j < 0:
                        if c == 0:
                            pe.wait_ge(x_in, 16)
                    else:
                        pe.wait_ge(x_ready, TC * j + c + 1)
                    xk = x[:, c, :].rearrange("p (m k) -> p k m", k=KD)
                    for half in range(2):
                        transposes(("xT", j, c, half), [xk[:, 4 * half + i, :] for i in range(4)])

            def wait_xT(j):
                pe.wait_ge(*drained(("xT", j, 1, 0)))
                pe.wait_ge(*drained(("xT", j, 1, 1)))

            def weights_unit(l, n, name, m0):
                pe.wait_ge(*landed(n))
                w = slot(n).rearrange("p (k c) -> p k c", k=KD)
                for m in range(2):
                    key = (name, l, m0 + m)
                    free(key)
                    for s in range(2):
                        at = (2 * m + s) * P
                        for k in range(KD):
                            last = nc.tensor.matmul(bank(key, T, s * T), w[:, k, at:at + P], xT[:, k, :],
                                                    start=(k == 0), stop=(k == KD - 1))
                    last.then_inc(bank_filled, 1)

            def tokens_unit(l, n, name, h):
                pe.wait_ge(*landed(n))
                w = slot(n).rearrange("p (k c) -> p k c", k=KD)
                for c in range(TC):
                    key = (name, l, h, c)
                    free(key)
                    for k in range(KD):
                        last = nc.tensor.matmul(bank(key), xT[:, k, c * P:(c + 1) * P], w[:, k, :],
                                                start=(k == 0), stop=(k == KD - 1))
                    last.then_inc(bank_filled, 1)

            def residual():
                for c in range(TC):
                    for h in range(NH):
                        nc.tensor.matmul(psum[:, 4 + NH * c + h, :], alpha_i, x[:, c, h * HB:(h + 1) * HB],
                                         start=True, stop=False, skip_group_check=True)

            def output_projection(l, lhs):
                for h in range(NH):
                    n = MOE_BASE[l] - NH + h
                    pe.wait_ge(*landed(n))
                    w = slot(n).rearrange("p (k c) -> p k c", k=KD)
                    for c in range(TC):
                        for k in range(KD):
                            last = nc.tensor.matmul(psum[:, 4 + NH * c + h, :], lhs[:, k, c * P:(c + 1) * P], w[:, k, :],
                                                    start=False, stop=(k == KD - 1), skip_group_check=True)
                        if h == NH - 1:
                            last.then_inc(z_ready, 1)
                    if h == 0:
                        last.then_inc(out_half0, 1)

            def o_transposes(l, ready):
                for c in range(TC):
                    pe.wait_ge(*ready(c))
                    for half in range(2):
                        transposes(("oT", l, c, half),
                                   [o_sb[:, c, (4 * half + i) * P:(4 * half + i + 1) * P] for i in range(4)])

            def attention(l, j):
                base = MIX_BASE[l]
                key = ("f", l)
                free(key)
                pe.wait_ge(wf_in, 32 * (j + 1))
                for c in range(TC):
                    for k in range(KD):
                        last = nc.tensor.matmul(bank(key, HEADS, c * HEADS), xT[:, k, c * P:(c + 1) * P], wf[:, k, :],
                                                start=(k == 0), stop=(k == KD - 1))
                last.then_inc(bank_filled, 1)
                for m in range(2):
                    weights_unit(l, base + m, "q", 2 * m)
                for m in range(2):
                    weights_unit(l, base + 2 + m, "k", 2 * m)
                key = ("cum", l)
                free(key)
                pe.wait_ge(lf_ready, j + 1)
                nc.tensor.matmul(psum[0:HEADS, FILLS.bank[key], 0:T], lf[:, 0, :],
                                 const[:, CONST_AT["tri"][0]:CONST_AT["ones"][1]], start=True, stop=False)
                nc.tensor.matmul(psum[0:HEADS, FILLS.bank[key], P:T], lf[:, 1, :], tri,
                                 start=False, stop=True).then_inc(bank_filled, 1)
                for m in range(2):
                    tokens_unit(l, base + 4 + m, "v", m)
                pe.wait_ge(*drained(("q", l, 3)))
                pe.wait_ge(*drained(("k", l, 3)))
                pe.wait_ge(*drained(("v", l, 1, 1)))
                pe.wait_ge(cum_in, 32 * (j + 1))
                for h in range(HEADS + 2):
                    if h < HEADS:
                        key = ("S", l, h)
                        free(key)
                        nc.tensor.matmul(bank(key, P), qa[0:66, h, 0:P], ka[0:66, h, 0:P], start=True, stop=True)
                        nc.tensor.matmul(bank(key, T, P), qa[0:66, h, P:T], ka[0:66, h, :],
                                         start=True, stop=True).then_inc(bank_filled, 1)
                    if 1 <= h <= HEADS:
                        g = h - 1
                        key = ("PT", l, g)
                        free(key)
                        pe.wait_ge(p_ready, j * HEADS + g + 1)
                        for i in range(3):
                            last = nc.tensor.transpose(bank(key, P, i * P), pexp[:, g % 2, i * P:(i + 1) * P], ident)
                        last.then_inc(bank_filled, 1)
                    if h >= 2:
                        g = h - 2
                        key = ("O", l, g)
                        free(key)
                        pe.wait_ge(*drained(("PT", l, g)))
                        pair = slice((g // 2) * P, (g // 2 + 1) * P)
                        nc.tensor.matmul(bank(key, P), pT[:, g % 2, 0:P], v_sb[:, 0, pair], start=True, stop=True)
                        nc.tensor.matmul(bank(key, P, P), pT[:, g % 2, P:T], v_sb[:, 0, pair], start=True, stop=False)
                        nc.tensor.matmul(bank(key, P, P), pT[:, g % 2, T:3 * P], v_sb[:, 1, pair],
                                         start=False, stop=True).then_inc(bank_filled, 1)
                o_transposes(l, lambda c: drained(("O", l, HEADS - 1)))
                free(("z banks", l))
                residual()
                pe.wait_ge(*drained(("oT", l, 1, 0)))
                pe.wait_ge(*drained(("oT", l, 1, 1)))
                output_projection(l, xT)

            def hgrn(l):
                base = MIX_BASE[l]
                pe.wait_ge(diag_ready, 2)
                flat = lb_diag.rearrange("p s m k -> p s (m k)")
                for h in range(NH):
                    for s, name in enumerate(("lb", "omlb")):
                        free((name, l, h))
                        nc.tensor.matmul(bank((name, l, h)), ones, flat[:, s, h * HB:(h + 1) * HB],
                                         start=True, stop=True).then_inc(bank_filled, 1)
                for m in range(2):
                    tokens_unit(l, base + m, "fg", m)
                for m in range(2):
                    weights_unit(l, base + 2 + m, "q", 2 * m)
                for c in range(TC):
                    for half in range(2):
                        pe.wait_ge(fg_ready, TC * half + c + 1)
                        transposes(("kT", l, c, half),
                                   [fg[:, c, (4 * half + i) * P:(4 * half + i + 1) * P] for i in range(4)])
                for m in range(2):
                    tokens_unit(l, base + 4 + m, "i", m)
                for m in range(2):
                    tokens_unit(l, base + 6 + m, "g", m)
                pe.wait_ge(*drained(("q", l, 3)))
                pe.wait_ge(log_ready, 4)
                pe.wait_ge(*drained(("i", l, 1, 1)))
                for h in range(HH + 2):
                    if h < HH:
                        for c in range(TC):
                            for b in range(2):
                                key = ("E", l, h, c, b)
                                free(key)
                                lfh = fg[:, c, h * P:(h + 1) * P]
                                if b == 0 or c == 0:
                                    last = nc.tensor.matmul(bank(key), lfh, spans[:, b * HB:(b + 1) * HB], start=True, stop=True)
                                else:
                                    nc.tensor.matmul(bank(key, 3 * P), lfh, spans[:, HB:HB + 3 * P], start=True, stop=True)
                                    last = nc.tensor.matmul(bank(key, P, 3 * P), lfh, tri, start=True, stop=True)
                                last.then_inc(bank_filled, 1)
                    if 1 <= h <= HH:
                        g = h - 1
                        pe.wait_ge(qd_ready, g + 1)
                        pe.wait_ge(kd_ready, g + 1)
                        key = ("X", l, g)
                        free(key)
                        nc.tensor.matmul(bank(key, P), qk[:, g % 2, 0, NL - 1, :], qk[:, g % 2, 1, NL - 1, :],
                                         start=True, stop=True).then_inc(bank_filled, 1)
                        for c in range(TC):
                            for b in range(2):
                                key = ("sc", l, g, c, b)
                                free(key)
                                for i in range(4):
                                    if 4 * b + i < NL - 1:
                                        kk = qq = qk[:, g % 2, c, 4 * b + i, :]
                                    else:
                                        kk, qq = kT[:, g, c * P:(c + 1) * P], qT[:, g, c * P:(c + 1) * P]
                                    last = nc.tensor.matmul(bank(key, P, i * P), kk, qq, start=True, stop=True)
                                last.then_inc(bank_filled, 1)
                    if h >= 2:
                        g = h - 2
                        key = ("pv", l, g)
                        free(key)
                        pe.wait_ge(*drained(("X", l, g)))
                        pe.wait_ge(sc_ready, TC * (g + 1))
                        ih = [i_sb[:, c, g * P:(g + 1) * P] for c in range(TC)]
                        nc.tensor.matmul(bank(key, P), scT[:, g % 2, 0, :], ih[0], start=True, stop=True)
                        nc.tensor.matmul(bank(key, P, P), scT[:, g % 2, 2, :], ih[0], start=True, stop=False)
                        nc.tensor.matmul(bank(key, P, P), scT[:, g % 2, 1, :], ih[1],
                                         start=False, stop=True).then_inc(bank_filled, 1)
                o_transposes(l, lambda c: (on_ready, c + 1))
                free(("z banks", l))
                residual()
                pe.wait_ge(*drained(("oT", l, 1, 0)))
                pe.wait_ge(*drained(("oT", l, 1, 1)))
                output_projection(l, xT)

            def convolution(l):
                base = MIX_BASE[l]
                for i, name in enumerate("bch"):
                    for m in range(2):
                        weights_unit(l, base + 2 * i + m, name, 2 * m)
                free(("z banks", l))
                residual()
                pe.wait_ge(y_conv, 4)
                output_projection(l, yT)

            def gather(sems, n, par, half):
                pe.wait_ge(sems["sel_ready"], n + 1)
                pe.wait_ge(sems["xw_ready"], n * 2 + (half + FREE))
                for i in range(4):
                    for c in range(TC):
                        xk = x[:, c, :].rearrange("p (m k) -> p k m", k=KD)[:, 4 * half + i, :]
                        last = nc.tensor.matmul(psum[:, 1, i * P:(i + 1) * P], xk, sel[:, par, c, :],
                                                start=(c == 0), stop=(c == TC - 1))
                last.then_inc(sems["gathered"], 1)

            def quad(sems, n, par, unit0, ready, ahead, last_quad):
                pe.wait_ge(sems["xw_ready"], n * 2 + (2 + FREE))
                pe.wait_ge(sems["h_ready"], n + FREE)
                for u in range(GU):
                    s = (unit0 + u) % RING
                    pe.wait_ge(*ready(s))
                    w = ring[:, s, :].rearrange("p (t e k f) -> p e k t f", t=2, e=QE, f=ED)
                    for kk in range(KD // GU):
                        k = u * (KD // GU) + kk
                        for e in range(QE):
                            rows = slice(W * e, W * (e + 1))
                            last = nc.tensor.matmul(psum[rows, 0, :].rearrange("p (t f) -> p t f", t=2),
                                                    xw[:, par, k, rows], w[:, e, kk],
                                                    start=(k == 0), stop=(k == KD - 1))
                    last.then_inc(sems["unit_used"], 1)
                if ahead:
                    gather(sems, n + 1, 1 - par, 0)
                pe.wait_ge(sems["h_ready"], n + (1 + FREE))
                pe.wait_ge(sems["y1_ready"], n + FREE)
                for i in range(FC):
                    nc.tensor.transpose(psum[:, 3, i * P:(i + 1) * P], h_sb[:, i * P:(i + 1) * P], ident)
                for c in range(TC):
                    last = nc.tensor.transpose(psum[:, 3, (FC + c) * P:(FC + c + 1) * P], selg[:, par, c, :], ident)
                last.then_inc(sems["hT_filled"], 1)
                if ahead:
                    gather(sems, n + 1, 1 - par, 1)
                pe.wait_ge(sems["hT_ready"], n + 1)
                pe.wait_ge(sems["y0_ready"], n + FREE)
                for j in range(FC):
                    s = (unit0 + GU + j) % RING
                    pe.wait_ge(*ready(s))
                    w = ring[:, s, :].rearrange("p (e c) -> p e c", e=QE)
                    for h in range(NH):
                        for e in range(QE):
                            rows = slice(W * e, W * (e + 1))
                            last = nc.tensor.matmul(psum[rows, 2 + h, :], hT[:, j, rows], w[:, e, h * HB:(h + 1) * HB],
                                                    start=(j == 0), stop=(j == FC - 1))
                        if h == 0 and j == FC - 1:
                            last.then_inc(sems["y_filled"], 1)
                    last.then_inc(sems["unit_used"], 1)
                pe.wait_ge(sems["y0_ready"], n + (1 + FREE))
                pe.wait_ge(sems["y1_ready"], n + (1 + FREE))
                for c in range(TC):
                    for h in range(NH):
                        last = nc.tensor.matmul(psum[:, 4 + NH * c + h, :], hT[:, FC + c, :], y_sb[:, h * HB:(h + 1) * HB],
                                                start=False, stop=last_quad, skip_group_check=True)
                    if last_quad and sems is first:
                        last.then_inc(z_ready, 1)
                if sems is more:
                    last.then_inc(more["combined"], 1)

            def experts(l):
                fills = [MOE_BASE[l] // RING + ((MOE_BASE[l] + u) % RING < MOE_BASE[l] % RING) for u in range(QU)]
                of_slot = {(MOE_BASE[l] + u) % RING: fills[u] for u in range(QU)}
                gather(first, l * NQ, 0, 0)
                gather(first, l * NQ, 0, 1)
                with pe.Fori(0, NQ // 2 - 1) as i:
                    for par in range(2):
                        quad(first, i * 2 + (l * NQ + par), par, MOE_BASE[l],
                             lambda s: (unit_in[s], i * 64 + 32 * (of_slot[s] + par + 1)), True, False)
                for par in range(2):
                    q = NQ - 2 + par
                    quad(first, l * NQ + q, par, MOE_BASE[l],
                         lambda s: (unit_in[s], 32 * (of_slot[s] + q + 1)), par == 0, par == 1)

            def experts_more(l, runs):
                with pe.Fori(0, NW - 1) as w:
                    with pe.Fori(0, NQ) as q:
                        n = runs * MORE + w * NQ + q
                        gather(more, n, 0, 0)
                        gather(more, n, 0, 1)
                        quad(more, n, 0, MOE_BASE[l], lambda s: (more_in[s], n * 32 + 32), False, True)

            x_transposes(-1)
            runs = 0
            for l in range(DEPTH):
                wait_xT(2 * l - 1)
                if KINDS[l] == 0:
                    attention(l, KINDS[:l].count(0))
                elif KINDS[l] == 1:
                    hgrn(l)
                else:
                    convolution(l)
                x_transposes(2 * l)
                wait_xT(2 * l)
                pe.wait_ge(w_r_in, 32 * (l + 1))
                key = ("logits", l)
                free(key)
                for c in range(TC):
                    for k in range(KD):
                        last = nc.tensor.matmul(bank(key, NG + NE, c * 64), xT[:, k, c * P:(c + 1) * P], w_router[:, k, :],
                                                start=(k == 0), stop=(k == KD - 1))
                last.then_inc(bank_filled, 1)
                residual()
                key = ("rank", l)
                free(key)
                pe.wait_ge(picked_ready, l + 1)
                nc.tensor.matmul(bank(key, NE), strict, picked[:, 0, :], start=True, stop=True)
                nc.tensor.matmul(bank(key, NE, NE), ones, picked[:, 0, :], start=True, stop=False)
                nc.tensor.matmul(bank(key, NE, NE), strict, picked[:, 1, :], start=False, stop=True)
                nc.tensor.matmul(bank(key, NE, 2 * NE), ones, picked[:, 0, :], start=True, stop=False)
                nc.tensor.matmul(bank(key, NE, 2 * NE), ones, picked[:, 1, :], start=False, stop=True).then_inc(bank_filled, 1)
                free(("moe banks", l))
                experts(l)
                runs = more_path(pe, l, runs, experts_more)
                if l < DEPTH - 1:
                    x_transposes(2 * l + 1)

        @block.scalar
        def _(act):
            act.dma_start(x[:], a["x"][0].rearrange("(c p) d -> p c d", p=P)).then_inc(x_in, 16)
            act.dma_start(const[:], a["const"]).then_inc(const_in, 16)
            steps = [0]

            def step(ins):
                steps[0] += 1
                ins.then_inc(act_step, 1)
                act.wait_ge(act_step, steps[0])

            def drain(key, dst, src, func=ACT.Copy, **kw):
                act.wait_ge(*filled(key))
                nc.scalar.activation(dst, src, func, **kw).then_inc(drained_by["A"], 1)

            def x_drains(j):
                for c in range(TC):
                    for half in range(2):
                        key = ("xT", j, c, half)
                        if FILLS.drainer[key] == "A":
                            drain(key, xT[:, 4 * half:4 * half + 4, c * P:(c + 1) * P],
                                  bank(key).rearrange("p (k t) -> p k t", k=4))

            def o_drains(l):
                for c in range(TC):
                    key = ("oT", l, c, 0)
                    drain(key, xT[:, 0:4, c * P:(c + 1) * P], bank(key).rearrange("p (k t) -> p k t", k=4))

            def inverse_roots(of, mid, to, ready, n, done):
                act.wait_ge(ready, n)
                step(nc.scalar.activation(mid, of, ACT.Ln))
                nc.scalar.activation(to, mid, ACT.Exp, scale=-0.5).then_inc(done, 1)

            def norm(j):
                for c in range(TC):
                    inverse_roots(ve[:, c:c + 1], lnv[:, c:c + 1], rstd[:, c:c + 1], var_ready, TC * j + c + 1, seed_ready)

            def attention(l, j):
                act.wait_ge(lfz_ready, j + 1)
                step(nc.scalar.activation(lf_t, lf_z, ACT.Abs))
                step(nc.scalar.activation(lf_t, lf_t, ACT.Exp, scale=-1.0))
                nc.scalar.activation(lf_t, lf_t, ACT.Ln, bias=1.0).then_inc(lfe_ready, 1)
                for m in range(4):
                    key = ("q", l, m)
                    act.wait_ge(*filled(key))
                    for s in range(2):
                        ins = nc.scalar.activation(qa[0:HD, 4 * m + s:4 * m + s + 3:2, :],
                                                   psum[HD * s:HD * (s + 1), FILLS.bank[key], :].rearrange("p (m t) -> p m t", m=2),
                                                   ACT.Copy, scale=HD ** -0.5)
                    ins.then_inc(drained_by["A"], 1)
                for h in range(NH):
                    for c in range(TC):
                        drain(("v", l, h, c), v_sb[:, c, h * HB:(h + 1) * HB], bank(("v", l, h, c)))
                for h in range(HEADS + 1):
                    if h < HEADS:
                        act.wait_ge(nmax_ready, j * HEADS + h + 1)
                        for c in range(TC):
                            cols = slice(0, P) if c == 0 else slice(P, 3 * P)
                            ins = nc.scalar.activation(pexp[:, h % 2, cols], sm[:, h % 2, cols], ACT.Exp, scale=-1.0,
                                                       bias=nmax[:, h % 2, c:c + 1], accum_out=psums[:, h, c:c + 1])
                        ins.then_inc(p_ready, 1)
                    if h >= 1:
                        drain(("PT", l, h - 1), pT[:, (h - 1) % 2, :], bank(("PT", l, h - 1), 3 * P))
                o_drains(l)

            def hgrn(l):
                for h in range(NH):
                    for s, name in enumerate(("lb", "omlb")):
                        drain((name, l, h), lbs[:, s, h * HB:(h + 1) * HB], bank((name, l, h)))
                for h in range(NH):
                    for c in range(TC):
                        drain(("fg", l, h, c), fg[:, c, h * HB:(h + 1) * HB], bank(("fg", l, h, c)), ACT.Sigmoid)
                for m in range(4):
                    drain(("q", l, m), qT[:, 2 * m:2 * m + 2, :], bank(("q", l, m)).rearrange("p (m t) -> p m t", m=2))
                for c in range(TC):
                    for half in range(2):
                        key = ("kT", l, c, half)
                        drain(key, kT[:, 4 * half:4 * half + 4, c * P:(c + 1) * P],
                              bank(key).rearrange("p (k t) -> p k t", k=4), ACT.Copy, scale=-1.0, bias=1.0)
                        f = fg[:, c, half * HB:(half + 1) * HB]
                        nc.scalar.activation(f, f, ACT.Ln).then_inc(log_ready, 1)
                for name, to, func in (("i", i_sb, ACT.Copy), ("g", sg_sb, ACT.Silu)):
                    for h in range(NH):
                        for c in range(TC):
                            drain((name, l, h, c), to[:, c, h * HB:(h + 1) * HB], bank((name, l, h, c)), func)
                for h in range(HH + 2):
                    if h < HH:
                        for c in range(TC):
                            for b in range(2):
                                key = ("E", l, h, c, b)
                                drain(key, qk[:, h % 2, c, 4 * b:4 * b + 4, :],
                                      bank(key).rearrange("p (i t) -> p i t", i=4), ACT.Exp)
                    if 1 <= h <= HH:
                        drain(("X", l, h - 1), scT[:, (h - 1) % 2, 2, :], bank(("X", l, h - 1), P))
                    if h >= 2:
                        g = h - 2
                        act.wait_ge(*filled(("pv", l, g)))
                        act.wait_ge(ssq_ready, g)
                        for c in range(TC):
                            ins = nc.scalar.activation(square[:, c, :], bank(("pv", l, g), P, c * P), ACT.Square,
                                                       accum_out=ssq[:, c, g:g + 1])
                        ins.then_inc(ssq_ready, 1)
                inverse_roots(ssq, ssq_t, rms, ssqe_ready, 1, rms_seed)
                o_drains(l)

            def convolution(l):
                for name, to in (("b", bT), ("c", cT)):
                    for m in range(4):
                        drain((name, l, m), to[:, 2 * m:2 * m + 2, :], bank((name, l, m)).rearrange("p (m t) -> p m t", m=2))

            def tokens(sems, n, par, half):
                act.wait_ge(sems["gathered"], n * 2 + half + 1)
                nc.scalar.activation(xw[:, par, 4 * half:4 * half + 4, :], psum[:, 1, :].rearrange("p (k s) -> p k s", k=4),
                                     ACT.Copy).then_inc(sems["xw_ready"], 1)

            def quad(sems, n, par, ahead):
                act.wait_ge(sems["unit_used"], n * QU + (GU + spare(sems)))
                nc.scalar.activation(silu_g, psum[:, 0, 0:ED], ACT.Silu).then_inc(sems["silu_ready"], 1)
                if ahead:
                    tokens(sems, n + 1, 1 - par, 0)
                    tokens(sems, n + 1, 1 - par, 1)
                act.wait_ge(sems["unit_used"], n * QU + (QU + spare(sems)))
                nc.scalar.activation(y_sb[:, HB:D], psum[:, 3, :], ACT.Copy).then_inc(sems["y1_ready"], 1)

            def experts(l):
                tokens(first, l * NQ, 0, 0)
                tokens(first, l * NQ, 0, 1)
                with act.Fori(0, NQ // 2 - 1) as i:
                    for par in range(2):
                        quad(first, i * 2 + (l * NQ + par), par, True)
                for par in range(2):
                    quad(first, l * NQ + NQ - 2 + par, par, par == 0)

            def experts_more(l, runs):
                with act.Fori(0, NW - 1) as w:
                    with act.Fori(0, NQ) as q:
                        n = runs * MORE + w * NQ + q
                        tokens(more, n, 0, 0)
                        tokens(more, n, 0, 1)
                        quad(more, n, 0, False)

            for sems in (first, more):
                act.sem_inc(sems["xw_ready"], FREE)
                act.sem_inc(sems["y1_ready"], FREE)
            act.wait_ge(lbx_ready, 1)
            nc.scalar.activation(lb_e, lb_e, ACT.Exp).then_inc(lbe_ready, 1)
            x_drains(-1)
            runs = 0
            for l in range(DEPTH):
                if KINDS[l] == 0:
                    attention(l, KINDS[:l].count(0))
                elif KINDS[l] == 1:
                    hgrn(l)
                else:
                    convolution(l)
                norm(2 * l)
                x_drains(2 * l)
                act.wait_ge(dge_ready, l + 1)
                nc.scalar.activation(ege, dge, ACT.Exp).then_inc(ege_ready, 1)
                experts(l)
                runs = more_path(act, l, runs, experts_more)
                norm(2 * l + 1)
                if l < DEPTH - 1:
                    x_drains(2 * l + 1)

        @block.vector
        def _(dve):
            v = nc.vector
            steps = [0]

            def step(ins):
                steps[0] += 1
                ins.then_inc(dve_step, 1)
                dve.wait_ge(dve_step, steps[0])

            def over(t, n):
                return t.unsqueeze(len(t.shape)).to_broadcast([*t.shape, n])

            def x_drains(j):
                key = ("xT", j, 1, 1)
                dve.wait_ge(*filled(key))
                v.tensor_copy(xT[:, 4:8, P:T], bank(key).rearrange("p (k t) -> p k t", k=4)).then_inc(drained_by["V"], 1)

            def o_drains(l):
                for c in range(TC):
                    key = ("oT", l, c, 1)
                    dve.wait_ge(*filled(key))
                    v.tensor_copy(xT[:, 4:8, c * P:(c + 1) * P],
                                  bank(key).rearrange("p (k t) -> p k t", k=4)).then_inc(drained_by["V"], 1)

            def refine(y, val, tmp):
                step(v.tensor_tensor(tmp, y, y, ALU.mult))
                step(v.tensor_tensor(tmp, tmp, val, ALU.mult))
                step(v.tensor_scalar(tmp, tmp, -0.5, 1.5, ALU.mult, ALU.add))
                step(v.tensor_tensor(y, y, tmp, ALU.mult))

            def norm(j):
                dve.wait_ge(affine_in, 32 * (j + 1))
                for c in range(TC):
                    dve.wait_ge(z_ready, TC * j + c + 1)
                    z = [psum[:, 4 + NH * c + h, :] for h in range(NH)]
                    v.bn_stats(stats[:, c, 0, :], z[0])
                    step(v.bn_stats(stats[:, c, 1, :], z[1]))
                    step(v.bn_aggr(mv[:, c, :], stats[:, c, :, :]))
                    v.tensor_scalar(ve[:, c:c + 1], mv[:, c, 1:2], LN_EPS, None, ALU.add).then_inc(var_ready, 1)
                    for h in range(NH):
                        ins = v.scalar_tensor_tensor(out=x[:, c, h * HB:(h + 1) * HB], in0=z[h], scalar=mv[:, c, 0:1],
                                                     in1=affine[:, 0, h * HB:(h + 1) * HB], op0=ALU.subtract, op1=ALU.mult)
                    step(ins)
                    dve.wait_ge(seed_ready, TC * j + c + 1)
                    refine(rstd[:, c:c + 1], ve[:, c:c + 1], nt[:, c:c + 1])
                    v.scalar_tensor_tensor(out=x[:, c, :], in0=x[:, c, :], scalar=rstd[:, c:c + 1], in1=affine[:, 1, :],
                                           op0=ALU.mult, op1=ALU.add).then_inc(x_ready, 1)

            def attention(l, j):
                key = ("f", l)
                dve.wait_ge(wf_in, 32 * (j + 1))
                dve.wait_ge(*filled(key))
                v.tensor_tensor(lf_z, bank(key, TC * HEADS).rearrange("p (c h) -> p c h", c=TC),
                                bf.unsqueeze(1).to_broadcast([P, TC, HEADS]), ALU.add).then_inc(drained_by["V"], 1)
                dve.wait_ge(*drained(key))
                v.tensor_scalar(lf, lf_z, 0.0, None, ALU.min).then_inc(lfz_ready, 1)
                dve.wait_ge(lfe_ready, j + 1)
                dve.wait_ge(lfz_ready, j + 1)
                v.tensor_tensor(lf, lf, lf_t, ALU.subtract).then_inc(lf_ready, 1)
                for m in range(4):
                    key = ("k", l, m)
                    dve.wait_ge(*filled(key))
                    for s in range(2):
                        ins = v.tensor_copy(ka[0:HD, 4 * m + s:4 * m + s + 3:2, :],
                                            psum[HD * s:HD * (s + 1), FILLS.bank[key], :].rearrange("p (m t) -> p m t", m=2))
                    ins.then_inc(drained_by["V"], 1)
                key = ("cum", l)
                dve.wait_ge(*filled(key))
                c16 = psum[0:HEADS, FILLS.bank[key], 0:T]
                v.tensor_copy(cum[0:HEADS, 0, :], c16)
                v.tensor_scalar(cum[0:HEADS, 1, :], c16, -1.0, None, ALU.mult).then_inc(drained_by["V"], 1)
                for h in range(HEADS + 2):
                    if h < HEADS:
                        key = ("S", l, h)
                        dve.wait_ge(*filled(key))
                        if h >= 2:
                            dve.wait_ge(p_ready, j * HEADS + h - 1)
                        s = sm[:, h % 2, :]
                        v.tensor_tensor(s, causal, bank(key, 3 * P), ALU.subtract).then_inc(drained_by["V"], 1)
                        dve.wait_ge(*drained(key))
                        v.tensor_reduce(nmax[:, h % 2, 0:1], s[:, 0:P], AX, ALU.min)
                        v.tensor_reduce(nmax[:, h % 2, 1:2], s[:, P:3 * P], AX, ALU.min).then_inc(nmax_ready, 1)
                    if h >= 2:
                        g = h - 2
                        key = ("O", l, g)
                        dve.wait_ge(p_ready, j * HEADS + g + 1)
                        step(v.reciprocal(rsum[:, g % 2, :], psums[:, g, :]))
                        dve.wait_ge(*filled(key))
                        for c in range(TC):
                            ins = v.tensor_scalar(o_sb[:, c, g * HD:(g + 1) * HD], bank(key, HD, c * P + (g % 2) * HD),
                                                  rsum[:, g % 2, c:c + 1], None, ALU.mult)
                        ins.then_inc(drained_by["V"], 1)
                o_drains(l)

            def lower_bounds():
                l = KINDS.index(1)
                dve.wait_ge(lb_in, 16)
                step(v.tensor_reduce(lb_m, lb_in_sb.rearrange("p r k -> p k r"), AX, ALU.max))
                v.tensor_tensor(lb_e, lb_in_sb, lb_m.unsqueeze(1).to_broadcast([P, DEPTH, KD]),
                                ALU.subtract).then_inc(lbx_ready, 1)
                dve.wait_ge(lbe_ready, 1)
                step(v.tensor_reduce(lb_s, lb_e.rearrange("p r k -> p k r"), AX, ALU.add))
                step(v.reciprocal(lb_s, lb_s))
                step(v.tensor_reduce(lb_m, lb_e[:, 1:l + 1, :].rearrange("p r k -> p k r"), AX, ALU.add))
                step(v.tensor_tensor(lb_v[:, 0, :], lb_m, lb_s, ALU.mult))
                step(v.tensor_scalar(lb_v[:, 1, :], lb_v[:, 0, :], -1.0, 1.0, ALU.mult, ALU.add))

            def hgrn(l):
                for s in range(2):
                    v.tensor_tensor(lb_diag[:, s].rearrange("p k m -> p (k m)").rearrange("p (m k) -> p m k", k=KD),
                                    over(ident, KD), lb_v[:, s, :].unsqueeze(1).to_broadcast([P, P, KD]),
                                    ALU.mult).then_inc(diag_ready, 1)
                for h in range(NH):
                    for c in range(TC):
                        f, cols = fg[:, c, h * HB:(h + 1) * HB], slice(h * HB, (h + 1) * HB)
                        dve.wait_ge(*drained(("fg", l, h, c)))
                        step(v.tensor_tensor(f, f, lbs[:, 1, cols], ALU.mult))
                        v.tensor_tensor(f, f, lbs[:, 0, cols], ALU.add).then_inc(fg_ready, 1)
                dve.wait_ge(norm_in, 16)
                for h in range(NH):
                    for c in range(TC):
                        g = sg_sb[:, c, h * HB:(h + 1) * HB].rearrange("p (h v) -> p h v", v=HK)
                        dve.wait_ge(*drained(("g", l, h, c)))
                        v.tensor_tensor(g, g, norm_g.unsqueeze(1).to_broadcast([P, 4, HK]), ALU.mult).then_inc(sg_ready, 1)
                dve.wait_ge(sg_ready, 4)
                for h in range(HH + 2):
                    if h < HH:
                        dve.wait_ge(*drained(("E", l, h, TC - 1, 1)))
                        for i, m in enumerate(LEVELS):
                            e = qk[:, h % 2, :, i, :].rearrange("p c (b s m) -> p c b s m", s=2, m=m)[:, :, :, 1, :]
                            q = qT[:, h, :].rearrange("p (c b s m) -> p c b s m", c=TC, s=2, m=m)[:, :, :, 1, :]
                            v.tensor_tensor(e, e, q, ALU.mult)
                        e = qk[:, h % 2, 1, NL - 1, :]
                        v.tensor_tensor(e, e, qT[:, h, P:T], ALU.mult).then_inc(qd_ready, 1)
                    if 1 <= h <= HH:
                        g = h - 1
                        for c in range(TC):
                            dve.wait_ge(sc_ready, TC * g + c)
                            for b in range(2):
                                key = ("sc", l, g, c, b)
                                dve.wait_ge(*filled(key))
                                v.tensor_tensor(masked[:, 4 * b:4 * b + 4, :], bank(key).rearrange("p (i t) -> p i t", i=4),
                                                masks.rearrange("p (i t) -> p i t", i=NL)[:, 4 * b:4 * b + 4, :],
                                                ALU.mult).then_inc(drained_by["V"], 1)
                            dve.wait_ge(*drained(key))
                            v.tensor_reduce(scT[:, g % 2, c, :], masked.rearrange("p i t -> p t i"), AX,
                                            ALU.add).then_inc(sc_ready, 1)
                    if h >= 2:
                        g = h - 2
                        key = ("pv", l, g)
                        dve.wait_ge(*filled(key))
                        dve.wait_ge(ssq_ready, g + 1)
                        cols = slice(g * HK, (g + 1) * HK)
                        v.tensor_tensor(o_sb[:, :, cols], bank(key, T).rearrange("p (c v) -> p c v", c=TC),
                                        sg_sb[:, :, cols], ALU.mult).then_inc(drained_by["V"], 1)
                dve.wait_ge(*drained(key))
                v.tensor_scalar(ssq, ssq, 1.0 / HK, RMS_EPS, ALU.mult, ALU.add).then_inc(ssqe_ready, 1)
                dve.wait_ge(ssqe_ready, 1)
                dve.wait_ge(rms_seed, 1)
                refine(rms, ssq, ssq_t)
                for c in range(TC):
                    o = o_sb[:, c, :].rearrange("p (h v) -> p h v", v=HK)
                    v.tensor_tensor(o, o, over(rms[:, c, :], HK), ALU.mult).then_inc(on_ready, 1)
                o_drains(l)

            def convolution(l):
                dve.wait_ge(taps_in, 16 * CW)
                dve.wait_ge(pad_set, 1)
                for m in range(4):
                    key = ("h", l, m)
                    two = slice(2 * m, 2 * m + 2)
                    dve.wait_ge(*drained(("c", l, m)))
                    dve.wait_ge(*filled(key))
                    v.tensor_tensor(zT[:, two, CW - 1:PADT], bank(key).rearrange("p (m t) -> p m t", m=2), cT[:, two, :],
                                    ALU.mult).then_inc(drained_by["V"], 1)
                    dve.wait_ge(*drained(key))
                    for w in range(CW):
                        for k in (2 * m, 2 * m + 1):
                            z, tap = zT[:, k, w:w + T], taps[:, w, k:k + 1]
                            if w == 0:
                                ins = v.tensor_scalar(yT[:, k, :], z, tap, None, ALU.mult)
                            else:
                                ins = v.scalar_tensor_tensor(out=yT[:, k, :], in0=z, scalar=tap, in1=yT[:, k, :],
                                                             op0=ALU.mult, op1=ALU.add)
                        step(ins)
                    v.tensor_tensor(yT[:, two, :], yT[:, two, :], bT[:, two, :], ALU.mult).then_inc(y_conv, 1)

            def first_best(of, n, onehot):
                step(v.tensor_reduce(gm, of, AX, ALU.max))
                step(v.tensor_tensor(eq[:, :, 0:n], of, over(gm, n), ALU.is_equal))
                step(v.tensor_tensor(vv[:, :, 0:n], eq[:, :, 0:n], rev[:, 0:n].unsqueeze(1).to_broadcast([P, TC, n]), ALU.mult))
                step(v.tensor_reduce(vm, vv[:, :, 0:n], AX, ALU.max))
                step(v.tensor_tensor(onehot, vv[:, :, 0:n], over(vm, n), ALU.is_equal))

            def both(group, expert):
                return over(group, EG), expert.unsqueeze(2).to_broadcast([P, TC, NG, EG])

            def grouped(t):
                return t.rearrange("p c (g e) -> p c g e", g=NG)

            def router(l):
                key = ("logits", l)
                if l == 0:
                    dve.wait_ge(b_in, 32)
                dve.wait_ge(*filled(key))
                v.tensor_tensor(lg, bank(key, P).rearrange("p (c e) -> p c e", c=TC)[:, :, 0:NG + NE],
                                b_router[:, l, :].unsqueeze(1).to_broadcast([P, TC, NG + NE]), ALU.add).then_inc(drained_by["V"], 1)
                dve.wait_ge(*drained(key))
                first_best(lg[:, :, 0:NG], NG, og)
                step(v.tensor_tensor(dge[:, :, 0:NG], lg[:, :, 0:NG], over(gm, NG), ALU.subtract))
                step(v.tensor_tensor(grouped(le), grouped(lg[:, :, NG:]), over(og, EG), ALU.mult))
                step(v.tensor_reduce(ig, grouped(le).rearrange("p c g e -> p c e g"), AX, ALU.add))
                first_best(ig, EG, o1)
                step(v.tensor_copy(m1, gm))
                step(v.scalar_tensor_tensor(out=ig, in0=o1, scalar=-BIG, in1=ig, op0=ALU.mult, op1=ALU.add))
                first_best(ig, EG, o2)
                v.tensor_tensor(dge[:, :, NG], gm, m1, ALU.subtract).then_inc(dge_ready, 1)
                for t, o in ((a1, o1), (a2, o2)):
                    g, e = both(og, o)
                    ins = v.tensor_tensor(grouped(t), g, e, ALU.mult)
                step(ins)
                v.tensor_tensor(picked, a1, a2, ALU.add).then_inc(picked_ready, 1)
                dve.wait_ge(ege_ready, l + 1)
                step(v.tensor_reduce(gsum, ege[:, :, 0:NG], AX, ALU.add))
                step(v.scalar_tensor_tensor(out=den, in0=ege[:, :, NG], scalar=1.0, in1=gsum, op0=ALU.add, op1=ALU.mult))
                step(v.reciprocal(w1, den))
                step(v.tensor_tensor(w2, w1, ege[:, :, NG], ALU.mult))
                v.tensor_tensor(a1, a1, over(w1, NE), ALU.mult)
                step(v.tensor_tensor(a2, a2, over(w2, NE), ALU.mult))
                step(v.tensor_tensor(gates, a1, a2, ALU.add))
                key = ("rank", l)
                dve.wait_ge(*filled(key))
                step(v.tensor_reduce(cmax, bank(key, NE, 2 * NE), AX, ALU.max))
                v.tensor_scalar(most[:, l:l + 1], cmax, float(WINDOW_LIMIT), None, ALU.is_gt).then_inc(most_ready, 1)
                v.scalar_tensor_tensor(out=rank, in0=bank(key, TC * NE).rearrange("p (c e) -> p c e", c=TC), scalar=1.0,
                                       in1=picked, op0=ALU.add, op1=ALU.mult).then_inc(drained_by["V"], 1)
                dve.wait_ge(*drained(key))
                step(v.tensor_scalar(rank, rank, -1.0, None, ALU.add))

            def select(sems, n, e0, par):
                if sems is first:
                    dve.wait_ge(sems["hT_filled"], n + (FREE - 1))
                s = sel[:, par].rearrange("p c (e w) -> p c e w", e=QE)
                g = selg[:, par].rearrange("p c (e w) -> p c e w", e=QE)
                v.tensor_tensor(s, over(rank[:, :, bass.ds(e0, QE)], W),
                                iota.unsqueeze(1).unsqueeze(1).to_broadcast([P, TC, QE, W]),
                                ALU.is_equal).then_inc(sems["sel_made"], 1)
                dve.wait_ge(sems["sel_made"], n + 1)
                v.tensor_tensor(g, s, over(gates[:, :, bass.ds(e0, QE)], W), ALU.mult).then_inc(sems["sel_ready"], 1)

            def quad(sems, n, ahead):
                if ahead:
                    ahead()
                dve.wait_ge(sems["silu_ready"], n + 1)
                v.tensor_tensor(h_sb, silu_g, psum[:, 0, ED:2 * ED], ALU.mult).then_inc(sems["h_ready"], 1)
                dve.wait_ge(sems["hT_filled"], n + (1 + FREE))
                v.tensor_copy(hT, psum[:, 3, :].rearrange("p (i s) -> p i s", i=FC + TC)).then_inc(sems["hT_ready"], 1)
                dve.wait_ge(sems["y_filled"], n + 1)
                v.tensor_copy(y_sb[:, 0:HB], psum[:, 2, :]).then_inc(sems["y0_ready"], 1)

            def experts(l):
                n0 = l * NQ
                select(first, n0, 0, 0)
                with dve.Fori(0, NQ // 2 - 1) as i:
                    for par in range(2):
                        quad(first, i * 2 + (n0 + par),
                             lambda: select(first, i * 2 + (n0 + par + 1), i * (2 * QE) + (par + 1) * QE, 1 - par))
                for par in range(2):
                    q = NQ - 2 + par
                    quad(first, n0 + q, (lambda: select(first, n0 + q + 1, (q + 1) * QE, 1 - par)) if par == 0 else None)

            def experts_more(l, runs):
                dve.wait_ge(z_ready, TC * (2 * l + 2))
                with dve.Fori(0, NW - 1) as w:
                    v.tensor_scalar(rank, rank, float(-W), None, ALU.add).then_inc(more["shifted"], 1)
                    with dve.Fori(0, NQ) as q:
                        n = runs * MORE + w * NQ + q
                        dve.wait_ge(more["shifted"], runs * (NW - 1) + w + 1)
                        dve.wait_ge(more["combined"], n + FREE)
                        select(more, n, q * QE, 0)
                        quad(more, n, None)

            for sems in (first, more):
                dve.sem_inc(sems["h_ready"], FREE)
                dve.sem_inc(sems["y0_ready"], FREE)
            lower_bounds()
            x_drains(-1)
            runs = 0
            for l in range(DEPTH):
                if KINDS[l] == 0:
                    attention(l, KINDS[:l].count(0))
                elif KINDS[l] == 1:
                    hgrn(l)
                else:
                    convolution(l)
                norm(2 * l)
                x_drains(2 * l)
                router(l)
                experts(l)
                runs = more_path(dve, l, runs, experts_more)
                dve.wait_ge(more["combined"], runs * MORE + FREE)
                norm(2 * l + 1)
                if l < DEPTH - 1:
                    x_drains(2 * l + 1)


INS = ["x", "ln_mix_g", "ln_mix_b", "ln_ffn_g", "ln_ffn_b", "fox_w_in", "fox_b_f", "fox_w_out", "hgrn_w_in",
       "hgrn_lb_logits", "hgrn_norm_g", "hgrn_w_out", "conv_w_in", "conv_w", "conv_w_out", "moe_w_group", "moe_b_group",
       "moe_w_expert", "moe_b_expert", "moe_w_gate", "moe_w_up", "moe_w_down"]


def kernel(**inputs):
    import concourse.bacc as bacc
    from concourse.bass_utils import run_bass_kernel_spmd

    nc = bacc.Bacc("TRN2", target_bir_lowering=False, num_devices=1)
    arrays = {n: np.ascontiguousarray(inputs[n]) for n in INS}
    arrays["const"] = CONST
    aps = {n: nc.dram_tensor(f"in_{n}", v.shape, mybir.dt.from_np(v.dtype), kind="ExternalInput").ap() for n, v in arrays.items()}
    out = nc.dram_tensor("out", (1, T, D), F32, kind="ExternalOutput").ap()
    build(nc, aps, out)
    r = run_bass_kernel_spmd(nc, [{f"in_{n}": v for n, v in arrays.items()}], core_ids=[0])
    return r.results[0]["out"]
```

```python
import math
from contextlib import ExitStack

import numpy as np

import concourse.bass as bass
from concourse import mybir

F32 = mybir.dt.float32
I32 = mybir.dt.int32
ACT = mybir.ActivationFunctionType
ALU = mybir.AluOpType
AX = mybir.AxisListType.X

P = 128
D = 1024
KD = D // P
T = 256
TC = T // P
DEPTH = 4
HEADS, HD = 16, 64
HH, HK = 8, 128
CW = 3
NG, EG = 4, 8
NE = NG * EG
ED = 256
FC = ED // P
HB = 512
NH = D // HB
LN_EPS, RMS_EPS = 1e-5, 1e-6
ALPHA = float((2 * DEPTH) ** 0.25)
BIG = 1e30

QE = 4
W = P // QE
NQ = NE // QE
NW = T // W
GU = 4
QU = GU + FC

UNIT = 4096
RING = 6
assert QU % RING == 0
EARLY = 3
FIRST_EARLY = QU - EARLY
WINDOW_LIMIT = W
MORE = (NW - 1) * NQ
FREE = 1
KINDS = [layer % 3 for layer in range(DEPTH)]
IN_UNITS = {0: 6, 1: 8, 2: 6}
HGRN_ORDER = [2, 3, 0, 1, 4, 5, 6, 7]
MIX_UNITS = {k: n + NH for k, n in IN_UNITS.items()}
MIX_BASE = [sum(MIX_UNITS[k] for k in KINDS[:l]) + (NQ * QU - EARLY) * l for l in range(DEPTH)]
MOE_BASE = [MIX_BASE[l] + MIX_UNITS[KINDS[l]] for l in range(DEPTH)]

LEVELS = [64, 32, 16, 8, 4, 2, 1]
NL = len(LEVELS) + 1


def constants():
    i, j = np.arange(P)[:, None], np.arange(P)[None, :]
    parts = {
        "tri": i <= j, "ones": np.ones((P, P)), "strict": i < j,
        "alpha": np.eye(P) * ALPHA,
        "causal": np.concatenate([(j > i) * BIG, np.zeros((P, P)), (j > i) * BIG], 1),
        "iota": np.broadcast_to(np.arange(W), (P, W)),
        "rev": np.broadcast_to(EG - np.arange(EG), (P, EG)),
    }
    spans, masks = [], []
    for m in LEVELS:
        block_i, block_j = i // (2 * m), j // (2 * m)
        mid = block_j * 2 * m + m
        later = (j >= mid) & (i >= mid) & (i <= j)
        earlier = (j < mid) & (i > j) & (i < mid)
        spans.append(later | earlier)
        masks.append((block_i == block_j) & (i < mid) & (j >= mid))
    parts["spans"] = np.concatenate(spans + [i > j], 1)
    parts["masks"] = np.concatenate(masks, 1)
    parts["ident"] = np.eye(P)
    at, n = {}, 0
    for name, a in parts.items():
        at[name] = (n, n + a.shape[1])
        n += a.shape[1]
    return np.concatenate([np.asarray(a, np.float32) for a in parts.values()], 1), at


CONST, CONST_AT = constants()


EARLY_AT = 6160
O_AT = EARLY_AT + UNIT


class Fills:

    def __init__(self):
        self.no, self.bank, self.drainer, self.count = {}, {}, {}, {}
        self.of = {"A": 0, "V": 0}
        self.user, self.before = {}, {}

    def add(self, key, bank, drainer):
        self.no[key] = len(self.no) + 1
        self.bank[key], self.drainer[key] = bank, drainer
        self.of[drainer] += 1
        self.count[key] = self.of[drainer]
        self.before[key] = self.user.get(bank)
        self.user[bank] = key

    def mark(self, name, banks):
        self.before[name] = [self.user[b] for b in banks if b in self.user]


def plan():
    f = Fills()
    turn = [0]

    def rot(n, base=0):
        turn[0] += 1
        return base + turn[0] % n

    def transposed_x(j):
        for c in range(TC):
            for half in range(2):
                f.add(("xT", j, c, half), rot(4), "V" if (c, half) == (1, 1) else "A")

    transposed_x(-1)
    for l in range(DEPTH):
        kind = KINDS[l]
        if kind == 0:
            for name, drainer in (("q", "A"), ("k", "V")):
                for m in range(4):
                    f.add((name, l, m), rot(8), drainer)
                if name == "q":
                    f.add(("f", l), rot(8), "V")
            f.add(("cum", l), rot(8), "V")
            for h in range(NH):
                for c in range(TC):
                    f.add(("v", l, h, c), rot(8), "A")
            for h in range(HEADS + 3):
                if h < HEADS:
                    f.add(("S", l, h), rot(8), "V")
                if 2 <= h < HEADS + 2:
                    f.add(("PT", l, h - 2), rot(8), "A")
                if h >= 3:
                    f.add(("O", l, h - 3), rot(8), "V")
        elif kind == 1:
            for h in range(NH):
                f.add(("lb", l, h), rot(8), "A")
                f.add(("omlb", l, h), rot(8), "A")
            for h in range(NH):
                for c in range(TC):
                    f.add(("fg", l, h, c), rot(8), "A")
            for m in range(4):
                f.add(("q", l, m), rot(8), "A")
            for c in range(TC):
                for half in range(2):
                    f.add(("kT", l, c, half), rot(8), "A")
            for name in "ig":
                for h in range(NH):
                    for c in range(TC):
                        f.add((name, l, h, c), rot(8), "A")
            for h in range(HH + 2):
                if h < HH:
                    for c in range(TC):
                        for b in range(2):
                            f.add(("E", l, h, c, b), rot(8), "A")
                if 1 <= h <= HH:
                    f.add(("X", l, h - 1), rot(8), "A")
                    for c in range(TC):
                        for b in range(2):
                            f.add(("sc", l, h - 1, c, b), rot(8), "V")
                if h >= 2:
                    f.add(("pv", l, h - 2), rot(8), "V")
        else:
            for name, drainer in (("b", "A"), ("c", "A"), ("h", "V")):
                for m in range(4):
                    f.add((name, l, m), rot(8), drainer)
        if kind != 2:
            for c in range(TC):
                for half in range(2):
                    f.add(("oT", l, c, half), rot(4), "AV"[half])
        f.mark(("z banks", l), range(4, 8))
        transposed_x(2 * l)
        f.add(("logits", l), rot(4), "V")
        f.add(("rank", l), rot(4), "V")
        f.mark(("moe banks", l), range(4))
        if l < DEPTH - 1:
            transposed_x(2 * l + 1)
    return f


FILLS = plan()


def build(nc, a, out):
    with ExitStack() as ctx:
        def sb(name, shape, dt=F32):
            return ctx.enter_context(nc.sbuf_tensor(name, shape, dt))

        def sem(name):
            return ctx.enter_context(nc.semaphore(name))

        ring = sb("ring", [P, RING, UNIT])
        x = sb("x", [P, TC, D])
        xT = sb("xT", [P, KD, T])
        affine = sb("affine", [P, 2, D])
        const = sb("const", [P, CONST.shape[1]])
        work = sb("work", [P, EARLY_AT + EARLY * UNIT])
        extra = work[:, O_AT + TC * D:]
        small = sb("small", [P, 512])
        w_router = sb("w_router", [P, KD, NG + NE])
        b_router = sb("b_router", [P, DEPTH, NG + NE])
        taps = sb("taps", [P, CW, KD])
        most = sb("most", [P, DEPTH], I32)
        psum = ctx.enter_context(nc.psum_tensor("psum", [P, 8, HB], F32))

        def table(name):
            return const[:, CONST_AT[name][0]:CONST_AT[name][1]]

        ident, ones, tri, strict = (table(n) for n in ("ident", "ones", "tri", "strict"))
        alpha_i, causal, iota, rev = (table(n) for n in ("alpha", "causal", "iota", "rev"))
        spans = table("spans")
        masks = const[:, CONST_AT["masks"][0]:CONST_AT["ident"][1]]

        def region(t, at, shape):
            n = int(np.prod(shape))
            v = t[:, at:at + n]
            if len(shape) == 1:
                return v
            names = "abcd"[:len(shape)]
            spec = f"p ({' '.join(names)}) -> p {' '.join(names)}"
            return v.rearrange(spec, **{k: s for k, s in zip(names[:-1], shape[:-1])})

        qa = region(work, 0, [HEADS, T])
        ka = region(work, 4096, [HEADS, T])
        v_sb = region(work, 8192, [TC, D])
        o_sb = region(work, O_AT, [TC, D])
        cum = region(work, O_AT, [2, T])
        lf = region(work, O_AT + 512, [TC, HEADS])
        lf_t = region(work, O_AT + 544, [TC, HEADS])
        lf_z = region(work, O_AT + 576, [TC, HEADS])
        wf = region(work, 5568, [KD, HEADS])
        bf = region(work, 5696, [HEADS])
        sm = region(extra, 0, [3, 384])
        pT = region(extra, 1152, [2, 384])
        psums = region(extra, 1920, [HEADS, TC])
        nmax = region(extra, 1952, [3, TC])
        rsum = region(extra, 1958, [2, TC])
        qT = region(work, 0, [HH, T])
        kT = region(work, 2048, [HH, T])
        fg = region(work, 4096, [TC, D])
        i_sb = region(work, 6144, [TC, D])
        sg_sb = region(work, 8192, [TC, D])
        lbs = region(work, O_AT, [2, D])
        lb_diag = region(work, 6144, [2, KD, P])
        qk = region(extra, 0, [2, TC, NL, P])
        masked = region(extra, 4096, [NL, P])
        scT = region(extra, 5120, [2, 3, P])
        square = region(extra, 5888, [TC, P])
        norm_g = region(small, 384, [HK])
        ssq = region(small, 336, [TC, HH])
        ssq_t = region(small, 352, [TC, HH])
        rms = region(small, 368, [TC, HH])
        bT = region(work, 0, [KD, T])
        PADT = T + CW - 1
        zT = region(work, 2048, [KD, PADT])
        yT = region(work, 2048 + KD * PADT, [KD, T])
        xw = region(work, 0, [2, KD, P])
        sel = region(work, 2048, [2, TC, P])
        selg = region(work, 2560, [2, TC, P])
        silu_g = region(work, 3072, [ED])
        h_sb = region(work, 3328, [ED])
        hT = region(work, 3584, [FC + TC, P])
        y_sb = region(work, 4096, [D])
        stats = region(small, 0, [TC, 2, 6])
        mv = region(small, 24, [TC, 2])
        ve = region(small, 28, [TC])
        lnv = region(small, 30, [TC])
        rstd = region(small, 32, [TC])
        nt = region(small, 34, [TC])
        lg = region(small, 40, [TC, NG + NE])
        gm = region(small, 112, [TC])
        eq = region(small, 114, [TC, EG])
        vm4 = region(small, 130, [TC, NG])
        vm = region(small, 146, [TC])
        og = region(small, 148, [TC, NG])
        m1 = region(small, 156, [TC, NG])
        m2 = region(small, 164, [TC, NG])
        dge = region(small, 208, [TC, NG + 1])
        ege = region(small, 218, [TC, NG + 1])
        gsum = region(small, 228, [TC])
        den = region(small, 230, [TC])
        w1 = region(small, 232, [TC])
        w2 = region(small, 234, [TC])
        cmax = region(small, 236, [1])
        lb_in_sb = region(small, 240, [DEPTH, KD])
        lb_e = region(small, 272, [DEPTH, KD])
        lb_m = region(small, 304, [KD])
        lb_s = region(small, 312, [KD])
        lb_v = region(small, 320, [2, KD])
        picked = region(work, 5120, [TC, NE])
        gates = region(work, 5184, [TC, NE])
        rank = region(work, 5248, [TC, NE])
        a1 = region(work, 5312, [TC, NE])
        a2 = region(work, 5376, [TC, NE])
        le = region(work, 5440, [TC, NE])
        ranks = region(work, 5504, [TC, NE])

        const_in, x_in, b_in, w_r_in, wf_in, taps_in, lb_in, cum_in, norm_in = (
            sem(n) for n in ("const_in", "x_in", "b_in", "w_r_in", "wf_in", "taps_in", "lb_in", "cum_in", "norm_in"))
        affine_in, tables_in = sem("affine_in"), sem("tables_in")
        early_in = [sem(f"early_in{s}") for s in range(EARLY)]
        unit_in = [sem(f"unit_in{s}") for s in range(RING)]
        unit_used, half_ready = sem("unit_used"), sem("half_ready")
        bank_filled = sem("bank_filled")
        drained_by = {"A": sem("drained_act"), "V": sem("drained_dve")}
        x_ready, z_ready = sem("x_ready"), sem("z_ready")
        var_ready, seed_ready = sem("var_ready"), sem("seed_ready")
        ones_set = sem("ones_set")
        dve_step, act_step = sem("dve_step"), sem("act_step")
        lfz_ready, lfe_ready, lf_ready = sem("lfz_ready"), sem("lfe_ready"), sem("lf_ready")
        nmax_ready, p_ready = sem("nmax_ready"), sem("p_ready")
        fg_ready, log_ready = sem("fg_ready"), sem("log_ready")
        lbx_ready, lbe_ready, diag_ready = sem("lbx_ready"), sem("lbe_ready"), sem("diag_ready")
        sg_ready, qd_ready, kd_ready, sc_ready, ssq_ready, on_ready = (
            sem(n) for n in ("sg_ready", "qd_ready", "kd_ready", "sc_ready", "ssq_ready", "on_ready"))
        ssqe_ready, rms_seed = sem("ssqe_ready"), sem("rms_seed")
        pad_set, y_conv = sem("pad_set"), sem("y_conv")
        dge_ready, ege_ready, picked_ready, most_ready = (sem(n) for n in ("dge_ready", "ege_ready", "picked_ready", "most_ready"))
        MOE = ("sel_ready", "gathered", "xw_ready", "silu_ready", "h_ready", "hT_filled", "hT_ready",
               "y0_ready", "y1_ready", "sel_made")
        first = {n: sem(f"{n}_1") for n in MOE}
        more = {n: sem(f"{n}_n") for n in MOE + ("combined", "shifted")}
        first["unit_used"], more["unit_used"] = unit_used, sem("unit_used_n")
        more_in = [sem(f"more_in{s}") for s in range(RING)]
        out_written = sem("out_written")

        def spare(sems):
            return FREE if sems is more else 0

        def filled(key):
            return bank_filled, FILLS.no[key]

        def drained(key):
            return drained_by[FILLS.drainer[key]], FILLS.count[key]

        def bank(key, n=HB, at=0):
            return psum[:, FILLS.bank[key], at:at + n]

        def landed(n):
            return unit_in[n % RING], 32 * (n // RING + 1)

        def slot(n):
            return ring[:, n % RING, :]

        def early_slot(u):
            return region(work, EARLY_AT + u * UNIT, [UNIT])

        def used(n):
            for l in range(DEPTH):
                if MOE_BASE[l] <= n < MOE_BASE[l] + NQ * QU - EARLY:
                    v = n - MOE_BASE[l]
                    return unit_used, NQ * QU * l + (v if v < FIRST_EARLY else v + EARLY) + 1
                if MIX_BASE[l] <= n < MOE_BASE[l]:
                    m, kind = n - MIX_BASE[l], KINDS[l]
                    if m >= IN_UNITS[kind]:
                        return (half_ready, 2 * l + 1) if m == IN_UNITS[kind] else (z_ready, TC * (2 * l + 1))
                    name = {0: "qqkkvv", 1: "ffqqiigg", 2: "bbcchh"}[kind][m]
                    if name in "vig" or (kind == 1 and name == "f"):
                        return filled((("fg" if name == "f" else name), l, m % 2, TC - 1))
                    return filled((name, l, 2 * (m % 2) + 1))

        def more_path(eng, l, runs, body):
            eng.wait_ge(most_ready, l + 1)
            over = eng.value_load(most[0:1, l:l + 1], min_val=0, max_val=1)
            with eng.If(over > 0):
                body(l, runs)
            return over + runs

        block = ctx.enter_context(nc.Block())

        @block.sync
        def _(sp):
            w_in = {0: a["fox_w_in"], 1: a["hgrn_w_in"], 2: a["conv_w_in"]}
            w_out = {0: a["fox_w_out"], 1: a["hgrn_w_out"], 2: a["conv_w_out"]}

            def mixer(l):
                kind, j = KINDS[l], KINDS[:l].count(KINDS[l])
                for m in range(MIX_UNITS[kind]):
                    n = MIX_BASE[l] + m
                    if m < IN_UNITS[kind]:
                        col = (HGRN_ORDER[m] if kind == 1 else m) * HB
                        src = w_in[kind][j].rearrange("(p k) c -> p k c", k=KD)[:, :, col:col + HB]
                    else:
                        col = (m - IN_UNITS[kind]) * HB
                        src = w_out[kind][j].rearrange("(k p) c -> p k c", p=P)[:, :, col:col + HB]
                    dst = slot(n).rearrange("p (k c) -> p k c", k=KD)
                    if n >= RING:
                        sp.wait_ge(*used(n - RING))
                    for g in range(2):
                        sp.dma_start(dst[:, 4 * g:4 * g + 4, :],
                                     src[:, 4 * g:4 * g + 4, :]).then_inc(unit_in[n % RING], 16)

            def quad_unit(l, e0, u, to, into):
                if u < GU:
                    dst = to.rearrange("p (t e k) -> p t e k", t=2, e=QE)
                    step = KD // GU * ED
                    for t, w in enumerate((a["moe_w_gate"], a["moe_w_up"])):
                        src = w[l, bass.ds(e0, QE)].rearrange("e (p k) f -> p e (k f)", p=P)
                        sp.dma_start(dst[:, t], src[:, :, u * step:(u + 1) * step]).then_inc(into, 16)
                else:
                    dst = to.rearrange("p (e j c) -> p e j c", e=QE, j=FC)
                    for g in (1, 0):
                        src = a["moe_w_down"][l, bass.ds(e0 + 2 * g, 2)].rearrange("e (j p) c -> p e j c", p=P)
                        sp.dma_start(dst[:, 2 * g:2 * g + 2], src[:, :, :, (u - GU) * HB:(u - GU + 1) * HB]).then_inc(into, 16)

            def early_unit(l, u):
                if KINDS[l] == 1:
                    sp.wait_ge(*filled(("oT", l, TC - 1, 1)))
                elif KINDS[l] == 0 and u < 2:
                    sp.wait_ge(*filled(("O", l, HEADS - 1) if u == 0 else ("oT", l, TC - 1, 1)))
                quad_unit(l, 0, FIRST_EARLY + u, early_slot(u), early_in[u])

            def experts(l):
                early_unit(l, EARLY - 1)
                for v in range(FIRST_EARLY + QU):
                    n = MOE_BASE[l] + v
                    if v == RING - NH:
                        for u in range(EARLY - 1):
                            early_unit(l, u)
                    sp.wait_ge(*used(n - RING))
                    if v < FIRST_EARLY:
                        quad_unit(l, 0, v, slot(n), unit_in[n % RING])
                    else:
                        quad_unit(l, QE, v - FIRST_EARLY, slot(n), unit_in[n % RING])
                with sp.Fori(2, NQ) as q:
                    for u in range(QU):
                        s = (MOE_BASE[l] + FIRST_EARLY + u) % RING
                        sp.wait_ge(unit_used, q * QU + (NQ * QU * l + u + 1 - RING))
                        quad_unit(l, q * QE, u, ring[:, s, :], unit_in[s])

            def experts_more(l, runs):
                sp.wait_ge(unit_used, NQ * QU * (l + 1))
                with sp.Fori(0, NW - 1) as w:
                    with sp.Fori(0, NQ) as q:
                        sp.wait_ge(more["unit_used"], runs * (MORE * QU) + w * (NQ * QU) + q * QU + FREE)
                        for u in range(QU):
                            s = (MOE_BASE[l] + u) % RING
                            quad_unit(l, q * QE, u, ring[:, s, :], more_in[s])

            sp.dma_start(x[:], a["x"][0].rearrange("(c p) d -> p c d", p=P)).then_inc(x_in, 16)
            tables = CONST_AT["ident"][0]
            sp.dma_start(const[:, tables:], a["const"][:, tables:]).then_inc(const_in, 16)
            runs = 0
            for l in range(DEPTH):
                mixer(l)
                experts(l)
                runs = more_path(sp, l, runs, experts_more)
                sp.wait_ge(more["unit_used"], runs * (MORE * QU) + FREE)
            for c in range(TC):
                sp.wait_ge(x_ready, TC * (2 * DEPTH - 1) + c + 1)
                sp.dma_start(out[0, c * P:(c + 1) * P, :], x[:, c, :]).then_inc(out_written, 16)
            sp.wait_ge(out_written, 16 * TC)

        @block.gpsimd
        def _(pool):
            def small_loads():
                pool.dma_start(lb_in_sb, a["hgrn_lb_logits"].rearrange("r (p k) -> p r k", k=KD)).then_inc(lb_in, 16)
                pool.dma_start(b_router[:, :, 0:NG], a["moe_b_group"].partition_broadcast(P)).then_inc(b_in, 16)
                pool.dma_start(b_router[:, :, NG:], a["moe_b_expert"].partition_broadcast(P)).then_inc(b_in, 16)
                pool.dma_start(norm_g, a["hgrn_norm_g"][0].partition_broadcast(P)).then_inc(norm_in, 16)
                for w in range(CW):
                    pool.dma_start(taps[:, w, :], a["conv_w"][0, w].rearrange("(k p) -> p k", p=P),
                                   allow_slow_non_contiguous=True).then_inc(taps_in, 16)

            def load_affine(j):
                l, names = j // 2, (("ln_mix_g", "ln_mix_b"), ("ln_ffn_g", "ln_ffn_b"))[j % 2]
                if j:
                    pool.wait_ge(x_ready, TC * j)
                for g, name in enumerate(names):
                    pool.dma_start(affine[:, g, :], a[name][l].partition_broadcast(P)).then_inc(affine_in, 16)

            for l in range(DEPTH):
                kind, j = KINDS[l], KINDS[:l].count(KINDS[l])
                if kind == 0:
                    pool.dma_start(wf, a["fox_w_in"][j].rearrange("(p k) c -> p k c", k=KD)[:, :, 3 * D:]).then_inc(wf_in, 16)
                    pool.dma_start(bf, a["fox_b_f"][j].partition_broadcast(P)).then_inc(wf_in, 16)
                if l == 0:
                    pool.wait_ge(*landed(0))
                    small_loads()
                load_affine(2 * l)
                if l:
                    pool.wait_ge(*filled(("logits", l - 1)))
                pool.dma_start(w_router[:, :, 0:NG], a["moe_w_group"][l].rearrange("(p k) c -> p k c", k=KD)).then_inc(w_r_in, 16)
                pool.dma_start(w_router[:, :, NG:], a["moe_w_expert"][l].rearrange("(p k) c -> p k c", k=KD)).then_inc(w_r_in, 16)
                if kind == 0:
                    nc.gpsimd.memset(qa[64:66, :, :], 1.0).then_inc(ones_set, 1)
                    pool.wait_ge(*drained(("f", l)))
                    nc.gpsimd.memset(ka[64:66, :, :], 1.0).then_inc(ones_set, 1)
                    pool.wait_ge(ones_set, 2 * (j + 1))
                    pool.wait_ge(*drained(("cum", l)))
                    pool.dma_start(qa[65:66, :, :], cum[0:HEADS, 0:1, :]).then_inc(cum_in, 16)
                    pool.dma_start(ka[64:65, :, :], cum[0:HEADS, 1:2, :]).then_inc(cum_in, 16)
                elif kind == 1:
                    for h in range(HH):
                        pool.wait_ge(*drained(("E", l, h, TC - 1, 1)))
                        for i, m in enumerate(LEVELS):
                            e = qk[:, h % 2, :, i, :].rearrange("p c (b s m) -> p c b s m", s=2, m=m)[:, :, :, 0, :]
                            k = kT[:, h, :].rearrange("p (c b s m) -> p c b s m", c=TC, s=2, m=m)[:, :, :, 0, :]
                            nc.gpsimd.tensor_tensor(e, e, k, ALU.mult)
                        e = qk[:, h % 2, 0, NL - 1, :]
                        nc.gpsimd.tensor_tensor(e, e, kT[:, h, 0:P], ALU.mult).then_inc(kd_ready, 1)
                else:
                    nc.gpsimd.memset(zT[:, :, 0:CW - 1], 0.0).then_inc(pad_set, 1)
                load_affine(2 * l + 1)

        @block.tensor
        def _(pe):
            for s in (first["hT_filled"], more["hT_filled"], more["unit_used"], more["combined"]):
                pe.sem_inc(s, FREE)
            pe.wait_ge(const_in, 16)

            def free(key):
                before = FILLS.before[key]
                for b in before if isinstance(before, list) else [before] if before else []:
                    pe.wait_ge(*drained(b))

            def transposes(key, parts):
                free(key)
                for i, t in enumerate(parts):
                    last = nc.tensor.transpose(bank(key, P, i * P), t, ident)
                last.then_inc(bank_filled, 1)

            def x_transposes(j, chunks=range(TC)):
                for c in chunks:
                    if j < 0:
                        if c == 0:
                            pe.wait_ge(x_in, 16)
                    else:
                        pe.wait_ge(x_ready, TC * j + c + 1)
                    xk = x[:, c, :].rearrange("p (m k) -> p k m", k=KD)
                    for half in range(2):
                        transposes(("xT", j, c, half), [xk[:, 4 * half + i, :] for i in range(4)])

            def wait_xT(j, c=TC - 1):
                pe.wait_ge(*drained(("xT", j, c, 0)))
                pe.wait_ge(*drained(("xT", j, c, 1)))

            def weights_unit(l, n, name, m0):
                pe.wait_ge(*landed(n))
                w = slot(n).rearrange("p (k c) -> p k c", k=KD)
                for m in range(2):
                    key = (name, l, m0 + m)
                    free(key)
                    for s in range(2):
                        at = (2 * m + s) * P
                        for k in range(KD):
                            last = nc.tensor.matmul(bank(key, T, s * T), w[:, k, at:at + P], xT[:, k, :],
                                                    start=(k == 0), stop=(k == KD - 1))
                    last.then_inc(bank_filled, 1)

            def tokens_unit(l, n, name, h):
                pe.wait_ge(*landed(n))
                w = slot(n).rearrange("p (k c) -> p k c", k=KD)
                for c in range(TC):
                    key = (name, l, h, c)
                    free(key)
                    for k in range(KD):
                        last = nc.tensor.matmul(bank(key), xT[:, k, c * P:(c + 1) * P], w[:, k, :],
                                                start=(k == 0), stop=(k == KD - 1))
                    last.then_inc(bank_filled, 1)

            def residual(chunks=range(TC)):
                for c in chunks:
                    for h in range(NH):
                        nc.tensor.matmul(psum[:, 4 + NH * c + h, :], alpha_i, x[:, c, h * HB:(h + 1) * HB],
                                         start=True, stop=False, skip_group_check=True)

            def output_projection(l, lhs):
                for h in range(NH):
                    n = MOE_BASE[l] - NH + h
                    pe.wait_ge(*landed(n))
                    w = slot(n).rearrange("p (k c) -> p k c", k=KD)
                    for c in range(TC):
                        for k in range(KD):
                            last = nc.tensor.matmul(psum[:, 4 + NH * c + h, :], lhs[:, k, c * P:(c + 1) * P], w[:, k, :],
                                                    start=False, stop=(k == KD - 1), skip_group_check=True)
                        if h == NH - 1:
                            last.then_inc(z_ready, 1)
                    if h == 0:
                        last.then_inc(half_ready, 1)

            def o_transposes(l, ready):
                for c in range(TC):
                    pe.wait_ge(*ready(c))
                    for half in range(2):
                        transposes(("oT", l, c, half),
                                   [o_sb[:, c, (4 * half + i) * P:(4 * half + i + 1) * P] for i in range(4)])

            def attention(l, j):
                base = MIX_BASE[l]
                for m in range(2):
                    weights_unit(l, base + m, "q", 2 * m)
                key = ("f", l)
                free(key)
                pe.wait_ge(wf_in, 32 * (j + 1))
                for c in range(TC):
                    for k in range(KD):
                        last = nc.tensor.matmul(bank(key, HEADS, c * HEADS), xT[:, k, c * P:(c + 1) * P], wf[:, k, :],
                                                start=(k == 0), stop=(k == KD - 1))
                last.then_inc(bank_filled, 1)
                for m in range(2):
                    weights_unit(l, base + 2 + m, "k", 2 * m)
                key = ("cum", l)
                free(key)
                pe.wait_ge(lf_ready, j + 1)
                pe.wait_ge(tables_in, 16)
                nc.tensor.matmul(psum[0:HEADS, FILLS.bank[key], 0:T], lf[:, 0, :],
                                 const[:, CONST_AT["tri"][0]:CONST_AT["ones"][1]], start=True, stop=False)
                nc.tensor.matmul(psum[0:HEADS, FILLS.bank[key], P:T], lf[:, 1, :], tri,
                                 start=False, stop=True).then_inc(bank_filled, 1)
                for m in range(2):
                    tokens_unit(l, base + 4 + m, "v", m)
                pe.wait_ge(*drained(("q", l, 3)))
                pe.wait_ge(*drained(("k", l, 3)))
                pe.wait_ge(*drained(("v", l, 1, 1)))
                pe.wait_ge(cum_in, 32 * (j + 1))
                for h in range(HEADS + 3):
                    if h < HEADS:
                        key = ("S", l, h)
                        free(key)
                        nc.tensor.matmul(bank(key, P), qa[0:66, h, 0:P], ka[0:66, h, 0:P], start=True, stop=True)
                        nc.tensor.matmul(bank(key, T, P), qa[0:66, h, P:T], ka[0:66, h, :],
                                         start=True, stop=True).then_inc(bank_filled, 1)
                    if 2 <= h < HEADS + 2:
                        g = h - 2
                        key = ("PT", l, g)
                        free(key)
                        pe.wait_ge(p_ready, j * HEADS + g + 1)
                        for i in range(3):
                            last = nc.tensor.transpose(bank(key, P, i * P), sm[:, g % 3, i * P:(i + 1) * P], ident)
                        last.then_inc(bank_filled, 1)
                    if h >= 3:
                        g = h - 3
                        key = ("O", l, g)
                        free(key)
                        pe.wait_ge(*drained(("PT", l, g)))
                        pair = slice((g // 2) * P, (g // 2 + 1) * P)
                        nc.tensor.matmul(bank(key, P), pT[:, g % 2, 0:P], v_sb[:, 0, pair], start=True, stop=True)
                        nc.tensor.matmul(bank(key, P, P), pT[:, g % 2, P:T], v_sb[:, 0, pair], start=True, stop=False)
                        nc.tensor.matmul(bank(key, P, P), pT[:, g % 2, T:3 * P], v_sb[:, 1, pair],
                                         start=False, stop=True).then_inc(bank_filled, 1)
                o_transposes(l, lambda c: drained(("O", l, HEADS - 1)))
                free(("z banks", l))
                residual()
                pe.wait_ge(*drained(("oT", l, 1, 0)))
                pe.wait_ge(*drained(("oT", l, 1, 1)))
                output_projection(l, xT)

            def hgrn(l):
                base = MIX_BASE[l]
                pe.wait_ge(diag_ready, 2)
                flat = lb_diag.rearrange("p s m k -> p s (m k)")
                for h in range(NH):
                    for s, name in enumerate(("lb", "omlb")):
                        free((name, l, h))
                        nc.tensor.matmul(bank((name, l, h)), ones, flat[:, s, h * HB:(h + 1) * HB],
                                         start=True, stop=True).then_inc(bank_filled, 1)
                for m in range(2):
                    tokens_unit(l, base + m, "fg", m)
                for m in range(2):
                    weights_unit(l, base + 2 + m, "q", 2 * m)
                for c in range(TC):
                    for half in range(2):
                        pe.wait_ge(fg_ready, TC * half + c + 1)
                        transposes(("kT", l, c, half),
                                   [fg[:, c, (4 * half + i) * P:(4 * half + i + 1) * P] for i in range(4)])
                for m in range(2):
                    tokens_unit(l, base + 4 + m, "i", m)
                for m in range(2):
                    tokens_unit(l, base + 6 + m, "g", m)
                pe.wait_ge(*drained(("q", l, 3)))
                pe.wait_ge(log_ready, 4)
                pe.wait_ge(*drained(("i", l, 1, 1)))
                for h in range(HH + 2):
                    if h < HH:
                        for c in range(TC):
                            for b in range(2):
                                key = ("E", l, h, c, b)
                                free(key)
                                lfh = fg[:, c, h * P:(h + 1) * P]
                                if b == 0 or c == 0:
                                    last = nc.tensor.matmul(bank(key), lfh, spans[:, b * HB:(b + 1) * HB], start=True, stop=True)
                                else:
                                    nc.tensor.matmul(bank(key, 3 * P), lfh, spans[:, HB:HB + 3 * P], start=True, stop=True)
                                    last = nc.tensor.matmul(bank(key, P, 3 * P), lfh, tri, start=True, stop=True)
                                last.then_inc(bank_filled, 1)
                    if 1 <= h <= HH:
                        g = h - 1
                        pe.wait_ge(qd_ready, g + 1)
                        pe.wait_ge(kd_ready, g + 1)
                        key = ("X", l, g)
                        free(key)
                        nc.tensor.matmul(bank(key, P), qk[:, g % 2, 0, NL - 1, :], qk[:, g % 2, 1, NL - 1, :],
                                         start=True, stop=True).then_inc(bank_filled, 1)
                        for c in range(TC):
                            for b in range(2):
                                key = ("sc", l, g, c, b)
                                free(key)
                                for i in range(4):
                                    if 4 * b + i < NL - 1:
                                        kk = qq = qk[:, g % 2, c, 4 * b + i, :]
                                    else:
                                        kk, qq = kT[:, g, c * P:(c + 1) * P], qT[:, g, c * P:(c + 1) * P]
                                    last = nc.tensor.matmul(bank(key, P, i * P), kk, qq, start=True, stop=True)
                                last.then_inc(bank_filled, 1)
                    if h >= 2:
                        g = h - 2
                        key = ("pv", l, g)
                        free(key)
                        pe.wait_ge(*drained(("X", l, g)))
                        pe.wait_ge(sc_ready, TC * (g + 1))
                        ih = [i_sb[:, c, g * P:(g + 1) * P] for c in range(TC)]
                        nc.tensor.matmul(bank(key, P), scT[:, g % 2, 0, :], ih[0], start=True, stop=True)
                        nc.tensor.matmul(bank(key, P, P), scT[:, g % 2, 2, :], ih[0], start=True, stop=False)
                        nc.tensor.matmul(bank(key, P, P), scT[:, g % 2, 1, :], ih[1],
                                         start=False, stop=True).then_inc(bank_filled, 1)
                o_transposes(l, lambda c: (on_ready, c + 1))
                free(("z banks", l))
                residual()
                pe.wait_ge(*drained(("oT", l, 1, 0)))
                pe.wait_ge(*drained(("oT", l, 1, 1)))
                output_projection(l, xT)

            def convolution(l):
                base = MIX_BASE[l]
                for i, name in enumerate("bch"):
                    for m in range(2):
                        weights_unit(l, base + 2 * i + m, name, 2 * m)
                free(("z banks", l))
                residual()
                pe.wait_ge(y_conv, 4)
                output_projection(l, yT)

            def gather(sems, n, par, half):
                pe.wait_ge(sems["sel_ready"], n + 1)
                pe.wait_ge(sems["xw_ready"], n * 2 + (half + FREE))
                for i in range(4):
                    for c in range(TC):
                        xk = x[:, c, :].rearrange("p (m k) -> p k m", k=KD)[:, 4 * half + i, :]
                        last = nc.tensor.matmul(psum[:, 1, i * P:(i + 1) * P], xk, sel[:, par, c, :],
                                                start=(c == 0), stop=(c == TC - 1))
                last.then_inc(sems["gathered"], 1)

            def quad(sems, n, par, slots, ahead, last_quad):
                pe.wait_ge(sems["h_ready"], n + FREE)
                for u in range(GU):
                    if u % (GU // 2) == 0:
                        pe.wait_ge(sems["xw_ready"], n * 2 + (u // (GU // 2) + 1 + FREE))
                    pe.wait_ge(*slots[u][1])
                    w = slots[u][0].rearrange("p (t e k f) -> p e k t f", t=2, e=QE, f=ED)
                    for kk in range(KD // GU):
                        k = u * (KD // GU) + kk
                        for e in range(QE):
                            rows = slice(W * e, W * (e + 1))
                            last = nc.tensor.matmul(psum[rows, 0, :].rearrange("p (t f) -> p t f", t=2),
                                                    xw[:, par, k, rows], w[:, e, kk],
                                                    start=(k == 0), stop=(k == KD - 1))
                    last.then_inc(sems["unit_used"], 1)
                if ahead:
                    gather(sems, n + 1, 1 - par, 0)
                pe.wait_ge(sems["h_ready"], n + (1 + FREE))
                pe.wait_ge(sems["y1_ready"], n + FREE)
                for i in range(FC):
                    nc.tensor.transpose(psum[:, 3, i * P:(i + 1) * P], h_sb[:, i * P:(i + 1) * P], ident)
                for c in range(TC):
                    last = nc.tensor.transpose(psum[:, 3, (FC + c) * P:(FC + c + 1) * P], selg[:, par, c, :], ident)
                last.then_inc(sems["hT_filled"], 1)
                if ahead:
                    gather(sems, n + 1, 1 - par, 1)
                pe.wait_ge(sems["hT_ready"], n + 1)
                pe.wait_ge(sems["y0_ready"], n + FREE)
                for h in range(NH):
                    pe.wait_ge(*slots[GU + h][1])
                    w = slots[GU + h][0].rearrange("p (e j c) -> p e j c", e=QE, j=FC)
                    for j in range(FC):
                        for e in range(QE):
                            rows = slice(W * e, W * (e + 1))
                            last = nc.tensor.matmul(psum[rows, 2 + h, :], hT[:, j, rows], w[:, e, j],
                                                    start=(j == 0), stop=(j == FC - 1))
                    last.then_inc(sems["unit_used"], 1)
                    pe.wait_ge(sems[("y0_ready", "y1_ready")[h]], n + (1 + FREE))
                    for c in range(TC):
                        last = nc.tensor.matmul(psum[:, 4 + NH * c + h, :], hT[:, FC + c, :], y_sb[:, h * HB:(h + 1) * HB],
                                                start=False, stop=last_quad, skip_group_check=True)
                        if last_quad and sems is first and h == NH - 1:
                            last.then_inc(z_ready, 1)
                    if last_quad and sems is first and h == 0:
                        last.then_inc(half_ready, 1)
                if sems is more:
                    last.then_inc(more["combined"], 1)

            def experts(l):
                unit1 = MOE_BASE[l] + FIRST_EARLY

                def in_ring(at, i=None):
                    return [(slot(at + u), landed(at + u) if i is None else (landed(at + u)[0], i * 64 + landed(at + u)[1]))
                            for u in range(QU)]

                gather(first, l * NQ, 0, 0)
                gather(first, l * NQ, 0, 1)
                early = [(early_slot(u), (early_in[u], 32 * (l + 1))) for u in range(EARLY)]
                quad(first, l * NQ, 0, in_ring(MOE_BASE[l])[:FIRST_EARLY] + early, True, False)
                with pe.Fori(0, NQ // 2 - 1) as i:
                    for p in range(2):
                        quad(first, i * 2 + (l * NQ + 1 + p), 1 - p, in_ring(unit1 + p * QU, i), True, False)
                quad(first, l * NQ + NQ - 1, 1, in_ring(unit1 + (NQ - 2) * QU), False, True)

            def experts_more(l, runs):
                with pe.Fori(0, NW - 1) as w:
                    with pe.Fori(0, NQ) as q:
                        n = runs * MORE + w * NQ + q
                        gather(more, n, 0, 0)
                        gather(more, n, 0, 1)
                        at = [(MOE_BASE[l] + u) % RING for u in range(QU)]
                        quad(more, n, 0, [(ring[:, s, :], (more_in[s], n * 32 + 32)) for s in at], False, True)

            x_transposes(-1)
            runs = 0
            for l in range(DEPTH):
                wait_xT(2 * l - 1)
                if KINDS[l] == 0:
                    attention(l, KINDS[:l].count(0))
                elif KINDS[l] == 1:
                    hgrn(l)
                else:
                    convolution(l)
                pe.wait_ge(w_r_in, 32 * (l + 1))
                for c in range(TC):
                    x_transposes(2 * l, [c])
                    wait_xT(2 * l, c)
                    if c == 0:
                        free(("logits", l))
                    for k in range(KD):
                        last = nc.tensor.matmul(bank(("logits", l), NG + NE, c * 64), xT[:, k, c * P:(c + 1) * P],
                                                w_router[:, k, :], start=(k == 0), stop=(k == KD - 1))
                    if c == TC - 1:
                        last.then_inc(bank_filled, 1)
                    residual([c])
                key = ("rank", l)
                free(key)
                pe.wait_ge(picked_ready, l + 1)
                nc.tensor.matmul(bank(key, NE), strict, picked[:, 0, :], start=True, stop=True)
                nc.tensor.matmul(bank(key, NE, NE), ones, picked[:, 0, :], start=True, stop=False)
                nc.tensor.matmul(bank(key, NE, NE), strict, picked[:, 1, :], start=False, stop=True)
                nc.tensor.matmul(bank(key, NE, 2 * NE), ones, picked[:, 0, :], start=True, stop=False)
                nc.tensor.matmul(bank(key, NE, 2 * NE), ones, picked[:, 1, :], start=False, stop=True).then_inc(bank_filled, 1)
                free(("moe banks", l))
                experts(l)
                runs = more_path(pe, l, runs, experts_more)
                if l < DEPTH - 1:
                    x_transposes(2 * l + 1)

        @block.scalar
        def _(act):
            steps = [0]

            def step(ins):
                steps[0] += 1
                ins.then_inc(act_step, 1)
                act.wait_ge(act_step, steps[0])

            def drain(key, dst, src, func=ACT.Copy, **kw):
                act.wait_ge(*filled(key))
                nc.scalar.activation(dst, src, func, **kw).then_inc(drained_by["A"], 1)

            def x_drains(j):
                for c in range(TC):
                    for half in range(2):
                        key = ("xT", j, c, half)
                        if FILLS.drainer[key] == "A":
                            drain(key, xT[:, 4 * half:4 * half + 4, c * P:(c + 1) * P],
                                  bank(key).rearrange("p (k t) -> p k t", k=4))

            def o_drains(l):
                for c in range(TC):
                    key = ("oT", l, c, 0)
                    drain(key, xT[:, 0:4, c * P:(c + 1) * P], bank(key).rearrange("p (k t) -> p k t", k=4))

            def inverse_roots(of, mid, to, ready, n, done):
                act.wait_ge(ready, n)
                step(nc.scalar.activation(mid, of, ACT.Ln))
                nc.scalar.activation(to, mid, ACT.Exp, scale=-0.5).then_inc(done, 1)

            def norm(j):
                for c in range(TC):
                    inverse_roots(ve[:, c:c + 1], lnv[:, c:c + 1], rstd[:, c:c + 1], var_ready, TC * j + c + 1, seed_ready)

            def attention(l, j):
                act.wait_ge(lfz_ready, j + 1)
                step(nc.scalar.activation(lf_t, lf_z, ACT.Abs))
                step(nc.scalar.activation(lf_t, lf_t, ACT.Exp, scale=-1.0))
                nc.scalar.activation(lf_t, lf_t, ACT.Ln, bias=1.0).then_inc(lfe_ready, 1)
                for m in range(4):
                    key = ("q", l, m)
                    act.wait_ge(*filled(key))
                    for s in range(2):
                        ins = nc.scalar.activation(qa[0:HD, 4 * m + s:4 * m + s + 3:2, :],
                                                   psum[HD * s:HD * (s + 1), FILLS.bank[key], :].rearrange("p (m t) -> p m t", m=2),
                                                   ACT.Copy, scale=HD ** -0.5)
                    ins.then_inc(drained_by["A"], 1)
                if l == 0:
                    act.wait_ge(lbx_ready, 1)
                    nc.scalar.activation(lb_e, lb_e, ACT.Exp).then_inc(lbe_ready, 1)
                for h in range(NH):
                    for c in range(TC):
                        drain(("v", l, h, c), v_sb[:, c, h * HB:(h + 1) * HB], bank(("v", l, h, c)))
                for h in range(HEADS + 2):
                    if h >= 2:
                        drain(("PT", l, h - 2), pT[:, h % 2, :], bank(("PT", l, h - 2), 3 * P))
                    if h < HEADS:
                        act.wait_ge(nmax_ready, j * HEADS + h + 1)
                        for c in range(TC):
                            cols = slice(0, P) if c == 0 else slice(P, 3 * P)
                            e = sm[:, h % 3, cols]
                            ins = nc.scalar.activation(e, e, ACT.Exp, scale=-1.0,
                                                       bias=nmax[:, h % 3, c:c + 1], accum_out=psums[:, h, c:c + 1])
                        ins.then_inc(p_ready, 1)
                o_drains(l)

            def hgrn(l):
                for h in range(NH):
                    for s, name in enumerate(("lb", "omlb")):
                        drain((name, l, h), lbs[:, s, h * HB:(h + 1) * HB], bank((name, l, h)))
                for h in range(NH):
                    for c in range(TC):
                        drain(("fg", l, h, c), fg[:, c, h * HB:(h + 1) * HB], bank(("fg", l, h, c)), ACT.Sigmoid)
                for m in range(4):
                    drain(("q", l, m), qT[:, 2 * m:2 * m + 2, :], bank(("q", l, m)).rearrange("p (m t) -> p m t", m=2))
                for c in range(TC):
                    for half in range(2):
                        key = ("kT", l, c, half)
                        drain(key, kT[:, 4 * half:4 * half + 4, c * P:(c + 1) * P],
                              bank(key).rearrange("p (k t) -> p k t", k=4), ACT.Copy, scale=-1.0, bias=1.0)
                        f = fg[:, c, half * HB:(half + 1) * HB]
                        nc.scalar.activation(f, f, ACT.Ln).then_inc(log_ready, 1)
                for name, to, func in (("i", i_sb, ACT.Copy), ("g", sg_sb, ACT.Silu)):
                    for h in range(NH):
                        for c in range(TC):
                            drain((name, l, h, c), to[:, c, h * HB:(h + 1) * HB], bank((name, l, h, c)), func)
                for h in range(HH + 2):
                    if h < HH:
                        for c in range(TC):
                            for b in range(2):
                                key = ("E", l, h, c, b)
                                drain(key, qk[:, h % 2, c, 4 * b:4 * b + 4, :],
                                      bank(key).rearrange("p (i t) -> p i t", i=4), ACT.Exp)
                    if 1 <= h <= HH:
                        drain(("X", l, h - 1), scT[:, (h - 1) % 2, 2, :], bank(("X", l, h - 1), P))
                    if h >= 2:
                        g = h - 2
                        act.wait_ge(*filled(("pv", l, g)))
                        act.wait_ge(ssq_ready, g)
                        for c in range(TC):
                            ins = nc.scalar.activation(square[:, c, :], bank(("pv", l, g), P, c * P), ACT.Square,
                                                       accum_out=ssq[:, c, g:g + 1])
                        ins.then_inc(ssq_ready, 1)
                inverse_roots(ssq, ssq_t, rms, ssqe_ready, 1, rms_seed)
                o_drains(l)

            def convolution(l):
                act.wait_ge(pad_set, 1)
                for name, to in (("b", bT), ("c", zT[:, :, CW - 1:PADT])):
                    for m in range(4):
                        drain((name, l, m), to[:, 2 * m:2 * m + 2, :], bank((name, l, m)).rearrange("p (m t) -> p m t", m=2))

            def tokens(sems, n, par, half):
                act.wait_ge(sems["gathered"], n * 2 + half + 1)
                nc.scalar.activation(xw[:, par, 4 * half:4 * half + 4, :], psum[:, 1, :].rearrange("p (k s) -> p k s", k=4),
                                     ACT.Copy).then_inc(sems["xw_ready"], 1)

            def quad(sems, n, par, ahead):
                act.wait_ge(sems["unit_used"], n * QU + (GU + spare(sems)))
                nc.scalar.activation(silu_g, psum[:, 0, 0:ED], ACT.Silu).then_inc(sems["silu_ready"], 1)
                if ahead:
                    tokens(sems, n + 1, 1 - par, 0)
                    tokens(sems, n + 1, 1 - par, 1)
                act.wait_ge(sems["unit_used"], n * QU + (QU + spare(sems)))
                nc.scalar.activation(y_sb[:, HB:D], psum[:, 3, :], ACT.Copy).then_inc(sems["y1_ready"], 1)

            def experts(l):
                tokens(first, l * NQ, 0, 0)
                tokens(first, l * NQ, 0, 1)
                with act.Fori(0, NQ // 2 - 1) as i:
                    for par in range(2):
                        quad(first, i * 2 + (l * NQ + par), par, True)
                for par in range(2):
                    quad(first, l * NQ + NQ - 2 + par, par, par == 0)

            def experts_more(l, runs):
                with act.Fori(0, NW - 1) as w:
                    with act.Fori(0, NQ) as q:
                        n = runs * MORE + w * NQ + q
                        tokens(more, n, 0, 0)
                        tokens(more, n, 0, 1)
                        quad(more, n, 0, False)

            for sems in (first, more):
                act.sem_inc(sems["xw_ready"], FREE)
                act.sem_inc(sems["y1_ready"], FREE)
            x_drains(-1)
            act.wait_ge(*landed(0))
            tables = CONST_AT["ident"][0]
            act.dma_start(const[:, 0:tables], a["const"][:, 0:tables]).then_inc(tables_in, 16)
            runs = 0
            for l in range(DEPTH):
                if KINDS[l] == 0:
                    attention(l, KINDS[:l].count(0))
                elif KINDS[l] == 1:
                    hgrn(l)
                else:
                    convolution(l)
                norm(2 * l)
                x_drains(2 * l)
                act.wait_ge(dge_ready, l + 1)
                nc.scalar.activation(ege, dge, ACT.Exp).then_inc(ege_ready, 1)
                experts(l)
                runs = more_path(act, l, runs, experts_more)
                norm(2 * l + 1)
                if l < DEPTH - 1:
                    x_drains(2 * l + 1)

        @block.vector
        def _(dve):
            v = nc.vector
            steps = [0]

            def step(ins):
                steps[0] += 1
                ins.then_inc(dve_step, 1)
                dve.wait_ge(dve_step, steps[0])

            def over(t, n):
                return t.unsqueeze(len(t.shape)).to_broadcast([*t.shape, n])

            def x_drains(j):
                key = ("xT", j, 1, 1)
                dve.wait_ge(*filled(key))
                v.tensor_copy(xT[:, 4:8, P:T], bank(key).rearrange("p (k t) -> p k t", k=4)).then_inc(drained_by["V"], 1)

            def o_drains(l):
                for c in range(TC):
                    key = ("oT", l, c, 1)
                    dve.wait_ge(*filled(key))
                    v.tensor_copy(xT[:, 4:8, c * P:(c + 1) * P],
                                  bank(key).rearrange("p (k t) -> p k t", k=4)).then_inc(drained_by["V"], 1)

            def refine(y, val, tmp):
                step(v.tensor_tensor(tmp, y, y, ALU.mult))
                step(v.tensor_tensor(tmp, tmp, val, ALU.mult))
                step(v.tensor_scalar(tmp, tmp, -0.5, 1.5, ALU.mult, ALU.add))
                step(v.tensor_tensor(y, y, tmp, ALU.mult))

            def norm(j):
                dve.wait_ge(affine_in, 32 * (j + 1))
                dve.wait_ge(half_ready, j + 1)
                for c in range(TC):
                    v.bn_stats(stats[:, c, 0, :], psum[:, 4 + NH * c, :])
                for c in range(TC):
                    dve.wait_ge(z_ready, TC * j + c + 1)
                    z = [psum[:, 4 + NH * c + h, :] for h in range(NH)]
                    step(v.bn_stats(stats[:, c, 1, :], z[1]))
                    step(v.bn_aggr(mv[:, c, :], stats[:, c, :, :]))
                    v.tensor_scalar(ve[:, c:c + 1], mv[:, c, 1:2], LN_EPS, None, ALU.add).then_inc(var_ready, 1)
                    for h in range(NH):
                        ins = v.scalar_tensor_tensor(out=x[:, c, h * HB:(h + 1) * HB], in0=z[h], scalar=mv[:, c, 0:1],
                                                     in1=affine[:, 0, h * HB:(h + 1) * HB], op0=ALU.subtract, op1=ALU.mult)
                    step(ins)
                    dve.wait_ge(seed_ready, TC * j + c + 1)
                    refine(rstd[:, c:c + 1], ve[:, c:c + 1], nt[:, c:c + 1])
                    v.scalar_tensor_tensor(out=x[:, c, :], in0=x[:, c, :], scalar=rstd[:, c:c + 1], in1=affine[:, 1, :],
                                           op0=ALU.mult, op1=ALU.add).then_inc(x_ready, 1)

            def attention(l, j):
                key = ("f", l)
                dve.wait_ge(wf_in, 32 * (j + 1))
                dve.wait_ge(*filled(key))
                v.tensor_tensor(lf_z, bank(key, TC * HEADS).rearrange("p (c h) -> p c h", c=TC),
                                bf.unsqueeze(1).to_broadcast([P, TC, HEADS]), ALU.add).then_inc(drained_by["V"], 1)
                dve.wait_ge(*drained(key))
                v.tensor_scalar(lf, lf_z, 0.0, None, ALU.min).then_inc(lfz_ready, 1)
                dve.wait_ge(lfe_ready, j + 1)
                dve.wait_ge(lfz_ready, j + 1)
                v.tensor_tensor(lf, lf, lf_t, ALU.subtract).then_inc(lf_ready, 1)
                for m in range(4):
                    key = ("k", l, m)
                    dve.wait_ge(*filled(key))
                    for s in range(2):
                        ins = v.tensor_copy(ka[0:HD, 4 * m + s:4 * m + s + 3:2, :],
                                            psum[HD * s:HD * (s + 1), FILLS.bank[key], :].rearrange("p (m t) -> p m t", m=2))
                    ins.then_inc(drained_by["V"], 1)
                key = ("cum", l)
                dve.wait_ge(*filled(key))
                c16 = psum[0:HEADS, FILLS.bank[key], 0:T]
                v.tensor_copy(cum[0:HEADS, 0, :], c16)
                v.tensor_scalar(cum[0:HEADS, 1, :], c16, -1.0, None, ALU.mult).then_inc(drained_by["V"], 1)
                if l == 0:
                    lower_bounds()
                for h in range(HEADS + 3):
                    if h < HEADS:
                        key = ("S", l, h)
                        dve.wait_ge(*filled(key))
                        if h >= 3:
                            dve.wait_ge(*filled(("PT", l, h - 3)))
                        s = sm[:, h % 3, :]
                        v.tensor_tensor(s, causal, bank(key, 3 * P), ALU.subtract).then_inc(drained_by["V"], 1)
                        dve.wait_ge(*drained(key))
                        v.tensor_reduce(nmax[:, h % 3, 0:1], s[:, 0:P], AX, ALU.min)
                        v.tensor_reduce(nmax[:, h % 3, 1:2], s[:, P:3 * P], AX, ALU.min).then_inc(nmax_ready, 1)
                    if h >= 3:
                        g = h - 3
                        key = ("O", l, g)
                        dve.wait_ge(p_ready, j * HEADS + g + 1)
                        step(v.reciprocal(rsum[:, g % 2, :], psums[:, g, :]))
                        dve.wait_ge(*filled(key))
                        for c in range(TC):
                            ins = v.tensor_scalar(o_sb[:, c, g * HD:(g + 1) * HD], bank(key, HD, c * P + (g % 2) * HD),
                                                  rsum[:, g % 2, c:c + 1], None, ALU.mult)
                        ins.then_inc(drained_by["V"], 1)
                o_drains(l)

            def lower_bounds():
                l = KINDS.index(1)
                dve.wait_ge(lb_in, 16)
                step(v.tensor_reduce(lb_m, lb_in_sb.rearrange("p r k -> p k r"), AX, ALU.max))
                v.tensor_tensor(lb_e, lb_in_sb, lb_m.unsqueeze(1).to_broadcast([P, DEPTH, KD]),
                                ALU.subtract).then_inc(lbx_ready, 1)
                dve.wait_ge(lbe_ready, 1)
                step(v.tensor_reduce(lb_s, lb_e.rearrange("p r k -> p k r"), AX, ALU.add))
                step(v.reciprocal(lb_s, lb_s))
                step(v.tensor_reduce(lb_m, lb_e[:, 1:l + 1, :].rearrange("p r k -> p k r"), AX, ALU.add))
                step(v.tensor_tensor(lb_v[:, 0, :], lb_m, lb_s, ALU.mult))
                step(v.tensor_scalar(lb_v[:, 1, :], lb_v[:, 0, :], -1.0, 1.0, ALU.mult, ALU.add))

            def hgrn(l):
                for s in range(2):
                    v.tensor_tensor(lb_diag[:, s].rearrange("p k m -> p (k m)").rearrange("p (m k) -> p m k", k=KD),
                                    over(ident, KD), lb_v[:, s, :].unsqueeze(1).to_broadcast([P, P, KD]),
                                    ALU.mult).then_inc(diag_ready, 1)
                for h in range(NH):
                    for c in range(TC):
                        f, cols = fg[:, c, h * HB:(h + 1) * HB], slice(h * HB, (h + 1) * HB)
                        dve.wait_ge(*drained(("fg", l, h, c)))
                        step(v.tensor_tensor(f, f, lbs[:, 1, cols], ALU.mult))
                        v.tensor_tensor(f, f, lbs[:, 0, cols], ALU.add).then_inc(fg_ready, 1)
                dve.wait_ge(norm_in, 16)
                for h in range(NH):
                    for c in range(TC):
                        g = sg_sb[:, c, h * HB:(h + 1) * HB].rearrange("p (h v) -> p h v", v=HK)
                        dve.wait_ge(*drained(("g", l, h, c)))
                        v.tensor_tensor(g, g, norm_g.unsqueeze(1).to_broadcast([P, 4, HK]), ALU.mult).then_inc(sg_ready, 1)
                dve.wait_ge(sg_ready, 4)
                for h in range(HH + 2):
                    if h < HH:
                        dve.wait_ge(*drained(("E", l, h, TC - 1, 1)))
                        for i, m in enumerate(LEVELS):
                            e = qk[:, h % 2, :, i, :].rearrange("p c (b s m) -> p c b s m", s=2, m=m)[:, :, :, 1, :]
                            q = qT[:, h, :].rearrange("p (c b s m) -> p c b s m", c=TC, s=2, m=m)[:, :, :, 1, :]
                            v.tensor_tensor(e, e, q, ALU.mult)
                        e = qk[:, h % 2, 1, NL - 1, :]
                        v.tensor_tensor(e, e, qT[:, h, P:T], ALU.mult).then_inc(qd_ready, 1)
                    if 1 <= h <= HH:
                        g = h - 1
                        for c in range(TC):
                            dve.wait_ge(sc_ready, TC * g + c)
                            for b in range(2):
                                key = ("sc", l, g, c, b)
                                dve.wait_ge(*filled(key))
                                v.tensor_tensor(masked[:, 4 * b:4 * b + 4, :], bank(key).rearrange("p (i t) -> p i t", i=4),
                                                masks.rearrange("p (i t) -> p i t", i=NL)[:, 4 * b:4 * b + 4, :],
                                                ALU.mult).then_inc(drained_by["V"], 1)
                            dve.wait_ge(*drained(key))
                            v.tensor_reduce(scT[:, g % 2, c, :], masked.rearrange("p i t -> p t i"), AX,
                                            ALU.add).then_inc(sc_ready, 1)
                    if h >= 2:
                        g = h - 2
                        key = ("pv", l, g)
                        dve.wait_ge(*filled(key))
                        dve.wait_ge(ssq_ready, g + 1)
                        cols = slice(g * HK, (g + 1) * HK)
                        v.tensor_tensor(o_sb[:, :, cols], bank(key, T).rearrange("p (c v) -> p c v", c=TC),
                                        sg_sb[:, :, cols], ALU.mult).then_inc(drained_by["V"], 1)
                dve.wait_ge(*drained(key))
                v.tensor_scalar(ssq, ssq, 1.0 / HK, RMS_EPS, ALU.mult, ALU.add).then_inc(ssqe_ready, 1)
                dve.wait_ge(ssqe_ready, 1)
                dve.wait_ge(rms_seed, 1)
                refine(rms, ssq, ssq_t)
                for c in range(TC):
                    o = o_sb[:, c, :].rearrange("p (h v) -> p h v", v=HK)
                    v.tensor_tensor(o, o, over(rms[:, c, :], HK), ALU.mult).then_inc(on_ready, 1)
                o_drains(l)

            def convolution(l):
                dve.wait_ge(taps_in, 16 * CW)
                dve.wait_ge(pad_set, 1)
                for m in range(4):
                    key = ("h", l, m)
                    two = slice(2 * m, 2 * m + 2)
                    dve.wait_ge(*drained(("c", l, m)))
                    dve.wait_ge(*filled(key))
                    v.tensor_tensor(zT[:, two, CW - 1:PADT], bank(key).rearrange("p (m t) -> p m t", m=2),
                                    zT[:, two, CW - 1:PADT],
                                    ALU.mult).then_inc(drained_by["V"], 1)
                    dve.wait_ge(*drained(key))
                    for w in range(CW):
                        for k in (2 * m, 2 * m + 1):
                            z, tap = zT[:, k, w:w + T], taps[:, w, k:k + 1]
                            if w == 0:
                                ins = v.tensor_scalar(yT[:, k, :], z, tap, None, ALU.mult)
                            else:
                                ins = v.scalar_tensor_tensor(out=yT[:, k, :], in0=z, scalar=tap, in1=yT[:, k, :],
                                                             op0=ALU.mult, op1=ALU.add)
                        step(ins)
                    v.tensor_tensor(yT[:, two, :], yT[:, two, :], bT[:, two, :], ALU.mult).then_inc(y_conv, 1)

            def first_best(*searches):
                for part in range(5):
                    for of, n, largest, at, ranks, onehot in searches:
                        if part == 0:
                            ins = v.tensor_reduce(largest, of, AX, ALU.max)
                        elif part == 1:
                            ins = v.tensor_tensor(ranks, of, over(largest, n), ALU.is_equal)
                        elif part == 2:
                            back = rev[:, 0:n].unsqueeze(1).unsqueeze(1).to_broadcast([P, TC, of.shape[2], n])
                            ins = v.tensor_tensor(ranks, ranks, back, ALU.mult)
                        elif part == 3:
                            ins = v.tensor_reduce(at, ranks, AX, ALU.max)
                        else:
                            ins = v.tensor_tensor(onehot, ranks, over(at, n), ALU.is_equal)
                    step(ins)

            def grouped(t):
                return t.rearrange("p c (g e) -> p c g e", g=NG)

            def router(l):
                key = ("logits", l)
                if l == 0:
                    dve.wait_ge(b_in, 32)
                dve.wait_ge(*filled(key))
                v.tensor_tensor(lg, bank(key, P).rearrange("p (c e) -> p c e", c=TC)[:, :, 0:NG + NE],
                                b_router[:, l, :].unsqueeze(1).to_broadcast([P, TC, NG + NE]), ALU.add).then_inc(drained_by["V"], 1)
                dve.wait_ge(*drained(key))
                le4 = grouped(lg[:, :, NG:])
                first_best((lg[:, :, 0:NG].unsqueeze(2), NG, gm.unsqueeze(2), vm.unsqueeze(2), eq[:, :, 0:NG].unsqueeze(2), og.unsqueeze(2)),
                           (le4, EG, m1, vm4, grouped(ranks), grouped(a1)))
                v.tensor_tensor(dge[:, :, 0:NG], lg[:, :, 0:NG], over(gm, NG), ALU.subtract)
                step(v.scalar_tensor_tensor(out=grouped(le), in0=grouped(a1), scalar=-BIG, in1=le4, op0=ALU.mult, op1=ALU.add))
                first_best((grouped(le), EG, m2, vm4, grouped(ranks), grouped(a2)))
                v.tensor_tensor(m2, m2, m1, ALU.subtract)
                v.tensor_tensor(grouped(a1), grouped(a1), over(og, EG), ALU.mult)
                step(v.tensor_tensor(grouped(a2), grouped(a2), over(og, EG), ALU.mult))
                v.tensor_tensor(picked, a1, a2, ALU.add).then_inc(picked_ready, 1)
                step(v.tensor_tensor(m2, m2, og, ALU.mult))
                v.tensor_reduce(dge[:, :, NG], m2, AX, ALU.add).then_inc(dge_ready, 1)
                dve.wait_ge(ege_ready, l + 1)
                step(v.tensor_reduce(gsum, ege[:, :, 0:NG], AX, ALU.add))
                step(v.scalar_tensor_tensor(out=den, in0=ege[:, :, NG], scalar=1.0, in1=gsum, op0=ALU.add, op1=ALU.mult))
                step(v.reciprocal(w1, den))
                step(v.tensor_tensor(w2, w1, ege[:, :, NG], ALU.mult))
                v.tensor_tensor(a1, a1, over(w1, NE), ALU.mult)
                step(v.tensor_tensor(a2, a2, over(w2, NE), ALU.mult))
                step(v.tensor_tensor(gates, a1, a2, ALU.add))
                key = ("rank", l)
                dve.wait_ge(*filled(key))
                step(v.tensor_reduce(cmax, bank(key, NE, 2 * NE), AX, ALU.max))
                v.tensor_scalar(most[:, l:l + 1], cmax, float(WINDOW_LIMIT), None, ALU.is_gt).then_inc(most_ready, 1)
                v.scalar_tensor_tensor(out=rank, in0=bank(key, TC * NE).rearrange("p (c e) -> p c e", c=TC), scalar=1.0,
                                       in1=picked, op0=ALU.add, op1=ALU.mult).then_inc(drained_by["V"], 1)
                dve.wait_ge(*drained(key))
                step(v.tensor_scalar(rank, rank, -1.0, None, ALU.add))

            def select(sems, n, e0, par):
                if sems is first:
                    dve.wait_ge(sems["hT_filled"], n + (FREE - 1))
                s = sel[:, par].rearrange("p c (e w) -> p c e w", e=QE)
                g = selg[:, par].rearrange("p c (e w) -> p c e w", e=QE)
                v.tensor_tensor(s, over(rank[:, :, bass.ds(e0, QE)], W),
                                iota.unsqueeze(1).unsqueeze(1).to_broadcast([P, TC, QE, W]),
                                ALU.is_equal).then_inc(sems["sel_made"], 1)
                dve.wait_ge(sems["sel_made"], n + 1)
                v.tensor_tensor(g, s, over(gates[:, :, bass.ds(e0, QE)], W), ALU.mult).then_inc(sems["sel_ready"], 1)

            def quad(sems, n, ahead):
                if ahead:
                    ahead()
                dve.wait_ge(sems["silu_ready"], n + 1)
                v.tensor_tensor(h_sb, silu_g, psum[:, 0, ED:2 * ED], ALU.mult).then_inc(sems["h_ready"], 1)
                dve.wait_ge(sems["hT_filled"], n + (1 + FREE))
                v.tensor_copy(hT, psum[:, 3, :].rearrange("p (i s) -> p i s", i=FC + TC)).then_inc(sems["hT_ready"], 1)
                dve.wait_ge(sems["unit_used"], n * QU + (GU + 1 + spare(sems)))
                v.tensor_copy(y_sb[:, 0:HB], psum[:, 2, :]).then_inc(sems["y0_ready"], 1)

            def experts(l):
                n0 = l * NQ
                select(first, n0, 0, 0)
                with dve.Fori(0, NQ // 2 - 1) as i:
                    for par in range(2):
                        quad(first, i * 2 + (n0 + par),
                             lambda: select(first, i * 2 + (n0 + par + 1), i * (2 * QE) + (par + 1) * QE, 1 - par))
                for par in range(2):
                    q = NQ - 2 + par
                    quad(first, n0 + q, (lambda: select(first, n0 + q + 1, (q + 1) * QE, 1 - par)) if par == 0 else None)

            def experts_more(l, runs):
                dve.wait_ge(z_ready, TC * (2 * l + 2))
                with dve.Fori(0, NW - 1) as w:
                    v.tensor_scalar(rank, rank, float(-W), None, ALU.add).then_inc(more["shifted"], 1)
                    with dve.Fori(0, NQ) as q:
                        n = runs * MORE + w * NQ + q
                        dve.wait_ge(more["shifted"], runs * (NW - 1) + w + 1)
                        dve.wait_ge(more["combined"], n + FREE)
                        select(more, n, q * QE, 0)
                        quad(more, n, None)

            for sems in (first, more):
                dve.sem_inc(sems["h_ready"], FREE)
                dve.sem_inc(sems["y0_ready"], FREE)
            x_drains(-1)
            runs = 0
            for l in range(DEPTH):
                if KINDS[l] == 0:
                    attention(l, KINDS[:l].count(0))
                elif KINDS[l] == 1:
                    hgrn(l)
                else:
                    convolution(l)
                norm(2 * l)
                x_drains(2 * l)
                router(l)
                experts(l)
                runs = more_path(dve, l, runs, experts_more)
                dve.wait_ge(more["combined"], runs * MORE + FREE)
                norm(2 * l + 1)
                if l < DEPTH - 1:
                    x_drains(2 * l + 1)


INS = ["x", "ln_mix_g", "ln_mix_b", "ln_ffn_g", "ln_ffn_b", "fox_w_in", "fox_b_f", "fox_w_out", "hgrn_w_in",
       "hgrn_lb_logits", "hgrn_norm_g", "hgrn_w_out", "conv_w_in", "conv_w", "conv_w_out", "moe_w_group", "moe_b_group",
       "moe_w_expert", "moe_b_expert", "moe_w_gate", "moe_w_up", "moe_w_down"]


def kernel(**inputs):
    import concourse.bacc as bacc
    from concourse.bass_utils import run_bass_kernel_spmd

    nc = bacc.Bacc("TRN2", target_bir_lowering=False, num_devices=1)
    arrays = {n: np.ascontiguousarray(inputs[n]) for n in INS}
    arrays["const"] = CONST
    aps = {n: nc.dram_tensor(f"in_{n}", v.shape, mybir.dt.from_np(v.dtype), kind="ExternalInput").ap() for n, v in arrays.items()}
    out = nc.dram_tensor("out", (1, T, D), F32, kind="ExternalOutput").ap()
    build(nc, aps, out)
    r = run_bass_kernel_spmd(nc, [{f"in_{n}": v for n, v in arrays.items()}], core_ids=[0])
    return r.results[0]["out"]
```
